# Optimizing a Trainium2 kernel written in Bass

```python
import jax
import jax.numpy as jnp
from jax import lax
import numpy as np

D_MODEL = 1024
BATCH = 1
SEQ = 256
DEPTH = 2
DEC_BATCH = 8
DEC_SEQ = 4
PAST_LEN = 2048
PAGE_SIZE = 128

POOL_WINDOWS = (2, 4, 8, 16)
N_POOL_GROUPS = len(POOL_WINDOWS)
POOL_GROUP = D_MODEL // 8
POOL_W = N_POOL_GROUPS * POOL_GROUP
POOL_STATE = max(POOL_WINDOWS) - 1
ATT_GROUPS = ((128, 1), (512, 4), (2048, 16))
N_ATT_GROUPS = len(ATT_GROUPS)
HEAD_DIM = 64
HEADS_PER_GROUP = D_MODEL // 128
N_ATT_HEADS = N_ATT_GROUPS * HEADS_PER_GROUP
GROUP_W = HEADS_PER_GROUP * HEAD_DIM
QKV_W = N_ATT_GROUPS * GROUP_W
ATT_OUT_W = GROUP_W
N_BRANCH = 2
IN_COLS = POOL_W + 3 * QKV_W + N_BRANCH * D_MODEL
Q_BLOCK = 128
ALIBI_MAX = 8.0
D_FF = ((8 * D_MODEL // 3 + 255) // 256) * 256
N_EXPERTS = 8
TOP_K = 2
D_FF_EXPERT = 7 * D_MODEL // 2
MOE_BLOCK_ROWS = 512
N_DENSE = (DEPTH + 1) // 2
N_MOE = DEPTH // 2
RMS_EPS = 1e-6
NEG_INF = -1e30

kernel_name = 'hybrid_pool_dilated_attn_decoder_step'

def rmsnorm(x, g):
    xf = x.astype(jnp.float32)
    y = xf * lax.rsqrt(jnp.mean(xf * xf, axis=-1, keepdims=True) + RMS_EPS)
    return (y * g.astype(jnp.float32)).astype(x.dtype)

def alibi_slopes():
    i = np.arange(1, N_ATT_HEADS + 1, dtype=np.float32)
    s = np.exp2(-ALIBI_MAX * i / N_ATT_HEADS).astype(np.float32)
    return jnp.asarray(s.reshape(N_ATT_GROUPS, HEADS_PER_GROUP))

def project(xn, w_in, q_gain, k_gain):
    b, l, _ = xn.shape
    z = xn @ w_in
    hs = (b, l, N_ATT_GROUPS, HEADS_PER_GROUP, HEAD_DIM)
    o = POOL_W
    u = z[..., :o]
    q = rmsnorm(z[..., o:o + QKV_W].reshape(hs), q_gain)
    k = rmsnorm(z[..., o + QKV_W:o + 2 * QKV_W].reshape(hs), k_gain)
    v = z[..., o + 2 * QKV_W:o + 3 * QKV_W].reshape(hs)
    gates = z[..., o + 3 * QKV_W:].reshape(b, l, N_BRANCH, D_MODEL)
    return u, q, k, v, gates

def causal_pool(u, pos):
    b, l, _ = u.shape
    uf = u.astype(jnp.float32)
    cp = jnp.concatenate([jnp.zeros((b, 1, POOL_W), jnp.float32), jnp.cumsum(uf, axis=1)], axis=1)
    means = []
    for gi, win in enumerate(POOL_WINDOWS):
        c = cp[..., gi * POOL_GROUP:(gi + 1) * POOL_GROUP]
        lagged = jnp.concatenate([jnp.zeros((b, win - 1, POOL_GROUP), jnp.float32), c[:, :l - win + 1]], axis=1)
        cnt = jnp.minimum(pos + 1, win).astype(jnp.float32)
        means.append((c[:, 1:] - lagged) / cnt[None, :, None])
    return jnp.concatenate(means, axis=-1) - uf

def pool_branch(u, pos, w_pool, pool_scale):
    b, l, _ = u.shape
    m = causal_pool(u, pos).reshape(b, l, N_POOL_GROUPS, POOL_GROUP)
    y = jnp.einsum('blgc,gcd->blgd', m, w_pool.astype(jnp.float32)).reshape(b, l, POOL_W)
    return (y * pool_scale.astype(jnp.float32)).astype(u.dtype)

def band_attention_prompt(q, k, v, dil, band, slopes):
    b, s, h, dh = q.shape
    l = s // dil
    nb = -(-l // Q_BLOCK)
    lp = nb * Q_BLOCK
    bb = b * dil

    def strided(t):
        return t.reshape(b, l, dil, h, dh).transpose(0, 2, 1, 3, 4).reshape(bb, l, h, dh).astype(jnp.float32)

    qs = jnp.pad(strided(q), ((0, 0), (0, lp - l), (0, 0), (0, 0))).reshape(bb, nb, Q_BLOCK, h, dh)

    def key_blocks(t):
        tp = jnp.pad(strided(t), ((0, 0), (Q_BLOCK, lp - l), (0, 0), (0, 0))).reshape(bb, nb + 1, Q_BLOCK, h, dh)
        return jnp.concatenate([tp[:, :-1], tp[:, 1:]], axis=2)

    kb, vb = key_blocks(k), key_blocks(v)
    qi = jnp.arange(Q_BLOCK)[:, None]
    kj = jnp.arange(2 * Q_BLOCK)[None, :]
    dist = qi - kj + Q_BLOCK
    key_idx = jnp.arange(nb)[:, None, None] * Q_BLOCK - Q_BLOCK + kj[None]
    valid = (dist >= 0) & (dist <= band) & (key_idx >= 0)
    sc = jnp.einsum('bnqhd,bnkhd->bnhqk', qs, kb) * (HEAD_DIM ** -0.5)
    sc = sc - slopes.astype(jnp.float32)[:, None, None] * (dist * dil).astype(jnp.float32)
    sc = jnp.where(valid[None, :, None], sc, NEG_INF)
    lse = jax.nn.logsumexp(sc, axis=-1)
    p = jnp.exp(sc - lse[..., None])
    o = jnp.einsum('bnhqk,bnkhd->bnqhd', p, vb).reshape(bb, lp, h, dh)[:, :l]
    o = o.reshape(b, dil, l, h, dh).transpose(0, 2, 1, 3, 4).reshape(b, s, h, dh)
    lse = lse.transpose(0, 1, 3, 2).reshape(bb, lp, h)[:, :l]
    lse = lse.reshape(b, dil, l, h).transpose(0, 2, 1, 3).reshape(b, s, h)
    return o, lse

def band_attention_sample(q, k_all, v_all, n_past, dil, band, slopes):
    t = q.shape[1]
    j = jnp.arange(band + 1)
    idx = n_past + jnp.arange(t)[:, None] - j[None, :] * dil
    valid = idx >= 0
    idx = jnp.maximum(idx, 0)
    kg = k_all[:, idx].astype(jnp.float32)
    vg = v_all[:, idx].astype(jnp.float32)
    sc = jnp.einsum('bthd,btjhd->bhtj', q.astype(jnp.float32), kg) * (HEAD_DIM ** -0.5)
    sc = sc - slopes.astype(jnp.float32)[:, None, None] * (j * dil).astype(jnp.float32)
    sc = jnp.where(valid, sc, NEG_INF)
    lse = jax.nn.logsumexp(sc, axis=-1)
    p = jnp.exp(sc - lse[..., None])
    o = jnp.einsum('bhtj,btjhd->bthd', p, vg)
    return o, lse.transpose(0, 2, 1)

def combine_groups(outs, lses):
    o = jnp.stack(outs, axis=0)
    w = jax.nn.softmax(jnp.stack(lses, axis=0), axis=0)
    y = jnp.sum(o * w[..., None], axis=0)
    return y.reshape(y.shape[0], y.shape[1], ATT_OUT_W)

def merge_branches(pool_o, att_o, gates, w_bp, w_ba, w_o):
    g = jax.nn.sigmoid(gates.astype(jnp.float32)).astype(pool_o.dtype)
    h = g[..., 0, :] * (pool_o @ w_bp) + g[..., 1, :] * (att_o @ w_ba)
    return h @ w_o

def swiglu_dense(x, w1, w3, w2):
    return (jax.nn.silu(x @ w1) * (x @ w3)) @ w2

def moe_rows_per_block(n_assign):
    r = 8
    while r < n_assign // N_EXPERTS and r < MOE_BLOCK_ROWS:
        r *= 2
    return r

def moe_swiglu(x, router_w, router_b, wg, wu, wd):
    shp = x.shape
    xf = x.reshape(-1, D_MODEL)
    n = xf.shape[0]
    logits = xf.astype(jnp.float32) @ router_w.astype(jnp.float32) + router_b.astype(jnp.float32)
    top_v, top_e = lax.top_k(logits, TOP_K)
    gate = jax.nn.softmax(top_v, axis=-1)
    a = n * TOP_K
    rows = moe_rows_per_block(a)
    n_blocks = -(-(a + N_EXPERTS * (rows - 1)) // rows)
    e_flat = top_e.reshape(-1)
    order = jnp.argsort(e_flat)
    e_sorted = e_flat[order]
    tok_sorted = (order // TOP_K).astype(jnp.int32)
    g_sorted = gate.reshape(-1)[order]
    counts = jnp.bincount(e_flat, length=N_EXPERTS)
    padded = (counts + rows - 1) // rows * rows
    start = jnp.cumsum(counts) - counts
    pend = jnp.cumsum(padded)
    pstart = pend - padded
    dest = pstart[e_sorted] + jnp.arange(a) - start[e_sorted]
    row_tok = jnp.full((n_blocks * rows,), n, dtype=jnp.int32).at[dest].set(tok_sorted)
    xb = jnp.concatenate([xf, jnp.zeros((1, D_MODEL), xf.dtype)], axis=0)[row_tok]
    xb = xb.reshape(n_blocks, rows, D_MODEL)
    blk_e = jnp.minimum(jnp.sum(jnp.arange(n_blocks)[:, None] * rows >= pend[None, :], axis=1), N_EXPERTS - 1)

    def expert_block(args):
        xblk, e = args
        return swiglu_dense(xblk, wg[e], wu[e], wd[e])

    yb = lax.map(expert_block, (xb, blk_e)).reshape(n_blocks * rows, D_MODEL)
    y = yb[dest] * g_sorted[:, None].astype(yb.dtype)
    out = jnp.zeros((n, D_MODEL), yb.dtype).at[tok_sorted].add(y)
    return out.reshape(shp)

def setup_inputs(seed: int = 0) -> dict:
    key = jax.random.key(seed)
    ks = jax.random.split(key, 32)
    f32 = jnp.float32

    def nrm(k, shape, scale):
        return jax.random.normal(k, shape, f32) * scale

    lw = [min(win, PAST_LEN) for win, _ in ATT_GROUPS]
    kvs = (HEADS_PER_GROUP, HEAD_DIM)
    return {
        'x_prompt': nrm(ks[0], (BATCH, SEQ, D_MODEL), 1.0),
        'x_sample': nrm(ks[1], (DEC_BATCH, DEC_SEQ, D_MODEL), 1.0),
        'state_pool': nrm(ks[2], (DEPTH, DEC_BATCH, POOL_STATE, POOL_W), 1.0),
        'cache_kv_g0': nrm(ks[3], (DEPTH, DEC_BATCH, lw[0], 2) + kvs, 1.0),
        'cache_kv_g1': nrm(ks[4], (DEPTH, DEC_BATCH, lw[1], 2) + kvs, 1.0),
        'cache_kv_g2': nrm(ks[5], (DEPTH, DEC_BATCH, lw[2], 2) + kvs, 1.0),
        'norm_attn': 1.0 + nrm(ks[6], (DEPTH, D_MODEL), 0.02),
        'w_in': nrm(ks[7], (DEPTH, D_MODEL, IN_COLS), D_MODEL ** -0.5),
        'q_norm': 1.0 + nrm(ks[8], (DEPTH, HEAD_DIM), 0.02),
        'k_norm': 1.0 + nrm(ks[9], (DEPTH, HEAD_DIM), 0.02),
        'w_pool': nrm(ks[10], (DEPTH, N_POOL_GROUPS, POOL_GROUP, POOL_GROUP), POOL_GROUP ** -0.5),
        'pool_scale': 1.0 + nrm(ks[11], (DEPTH, POOL_W), 0.02),
        'w_branch_pool': nrm(ks[12], (DEPTH, POOL_W, D_MODEL), POOL_W ** -0.5),
        'w_branch_attn': nrm(ks[13], (DEPTH, ATT_OUT_W, D_MODEL), ATT_OUT_W ** -0.5),
        'w_out': nrm(ks[14], (DEPTH, D_MODEL, D_MODEL), D_MODEL ** -0.5),
        'norm_ffn': 1.0 + nrm(ks[15], (DEPTH, D_MODEL), 0.02),
        'w1_dense': nrm(ks[16], (N_DENSE, D_MODEL, D_FF), D_MODEL ** -0.5),
        'w3_dense': nrm(ks[17], (N_DENSE, D_MODEL, D_FF), D_MODEL ** -0.5),
        'w2_dense': nrm(ks[18], (N_DENSE, D_FF, D_MODEL), D_FF ** -0.5),
        'router_w': nrm(ks[19], (N_MOE, D_MODEL, N_EXPERTS), D_MODEL ** -0.5),
        'router_b': nrm(ks[20], (N_MOE, N_EXPERTS), 0.01),
        'we_gate': nrm(ks[21], (N_MOE, N_EXPERTS, D_MODEL, D_FF_EXPERT), D_MODEL ** -0.5),
        'we_up': nrm(ks[22], (N_MOE, N_EXPERTS, D_MODEL, D_FF_EXPERT), D_MODEL ** -0.5),
        'we_down': nrm(ks[23], (N_MOE, N_EXPERTS, D_FF_EXPERT, D_MODEL), D_FF_EXPERT ** -0.5),
    }

def reference(x_prompt, x_sample, state_pool, cache_kv_g0, cache_kv_g1, cache_kv_g2,
              norm_attn, w_in, q_norm, k_norm, w_pool, pool_scale, w_branch_pool, w_branch_attn,
              w_out, norm_ffn, w1_dense, w3_dense, w2_dense, router_w, router_b,
              we_gate, we_up, we_down):
    slopes = alibi_slopes()
    caches = (cache_kv_g0, cache_kv_g1, cache_kv_g2)
    seq = x_prompt.shape[1]
    t_new = x_sample.shape[1]
    pos_p = jnp.arange(seq)
    pos_s = PAST_LEN - POOL_STATE + jnp.arange(POOL_STATE + t_new)
    xp, xs = x_prompt, x_sample
    pool_p, pool_s = [], []
    kv_p = [[] for _ in ATT_GROUPS]
    kv_s = [[] for _ in ATT_GROUPS]
    for layer in range(DEPTH):
        u, q, k, v, gates = project(rmsnorm(xp, norm_attn[layer]), w_in[layer], q_norm[layer], k_norm[layer])
        pool_o = pool_branch(u, pos_p, w_pool[layer], pool_scale[layer])
        outs, lses = [], []
        for gi, (win, dil) in enumerate(ATT_GROUPS):
            o, l = band_attention_prompt(q[:, :, gi], k[:, :, gi], v[:, :, gi], dil, win // dil, slopes[gi])
            outs.append(o)
            lses.append(l)
            keep = min(win, seq)
            kv_p[gi].append(jnp.stack([k[:, -keep:, gi], v[:, -keep:, gi]], axis=2))
        pool_p.append(u[:, -POOL_STATE:])
        att_o = combine_groups(outs, lses).astype(xp.dtype)
        xp = xp + merge_branches(pool_o, att_o, gates, w_branch_pool[layer], w_branch_attn[layer], w_out[layer])

        u, q, k, v, gates = project(rmsnorm(xs, norm_attn[layer]), w_in[layer], q_norm[layer], k_norm[layer])
        ext = jnp.concatenate([state_pool[layer].astype(u.dtype), u], axis=1)
        pool_o = pool_branch(ext, pos_s, w_pool[layer], pool_scale[layer])[:, POOL_STATE:]
        outs, lses = [], []
        for gi, (win, dil) in enumerate(ATT_GROUPS):
            c = caches[gi][layer].astype(k.dtype)
            n_past = c.shape[1]
            k_all = jnp.concatenate([c[:, :, 0], k[:, :, gi]], axis=1)
            v_all = jnp.concatenate([c[:, :, 1], v[:, :, gi]], axis=1)
            o, l = band_attention_sample(q[:, :, gi], k_all, v_all, n_past, dil, win // dil, slopes[gi])
            outs.append(o)
            lses.append(l)
            kv_s[gi].append(jnp.stack([k[:, :, gi], v[:, :, gi]], axis=2))
        pool_s.append(ext[:, -POOL_STATE:])
        att_o = combine_groups(outs, lses).astype(xs.dtype)
        xs = xs + merge_branches(pool_o, att_o, gates, w_branch_pool[layer], w_branch_attn[layer], w_out[layer])

        i = layer // 2
        if layer % 2 == 0:
            xp = xp + swiglu_dense(rmsnorm(xp, norm_ffn[layer]), w1_dense[i], w3_dense[i], w2_dense[i])
            xs = xs + swiglu_dense(rmsnorm(xs, norm_ffn[layer]), w1_dense[i], w3_dense[i], w2_dense[i])
        else:
            xp = xp + moe_swiglu(rmsnorm(xp, norm_ffn[layer]), router_w[i], router_b[i], we_gate[i], we_up[i], we_down[i])
            xs = xs + moe_swiglu(rmsnorm(xs, norm_ffn[layer]), router_w[i], router_b[i], we_gate[i], we_up[i], we_down[i])
    return (xp, xs,
            jnp.stack(pool_p), jnp.stack(pool_s),
            jnp.stack(kv_p[0]), jnp.stack(kv_s[0]),
            jnp.stack(kv_p[1]), jnp.stack(kv_s[1]),
            jnp.stack(kv_p[2]), jnp.stack(kv_s[2]))


_drawn_inputs = setup_inputs


def setup_inputs(seed=0):
    import zlib

    import numpy as np

    out = dict(_drawn_inputs(seed))
    spreads = {}
    factors = {'q_norm': 4.111, 'k_norm': 3.532, 'router_b': 2.983}
    for name, (base, spread) in spreads.items():
        noise = np.random.default_rng([zlib.crc32(name.encode()), seed]).standard_normal(out[name].shape)
        drawn = base * np.exp(spread * noise) if base else spread * noise
        out[name] = jnp.asarray(drawn.astype(out[name].dtype))
    for name, factor in factors.items():
        out[name] = (out[name] * factor).astype(out[name].dtype)
    return out
```

```python
import numpy as np
from contextlib import ExitStack
import concourse.bass as bass
from concourse import mybir
from concourse.alu_op_type import AluOpType as ALU

F32 = mybir.dt.float32
I32 = mybir.dt.int32
U32 = mybir.dt.uint32
F32R = mybir.dt.float32r
ACT = mybir.ActivationFunctionType
AX = mybir.AxisListType

PART = 128
D = 1024
KT = D // PART
SEQ, DB, DS = 256, 8, 4
NS = DB * DS
T = SEQ + NS
LAYERS = 2
H, HD, G = 8, 64, 3
GW = H * HD
J = GW // PART
QKV = G * GW
POOL_W = 512
PG = POOL_W // PART
IN_COLS = POOL_W + 3 * QKV + 2 * D
WINDOWS = (2, 4, 8, 16)
DIL = (1, 4, 16)
SPAN = (128, 512, 2048)
PAST = 2048
STATE = 15
FF = 2816
FT = FF // PART
NE, FE = 8, 3584
ET = FE // PART
EPS = 1e-6
MASKED = 1e33
NEG = -1e30

CH = 2048
RING = 5
MRING = 7
SRING = 2
MSRING = 3
HB = 2
BH = DB // HB
ROWS = BH * DS * H
TT = ((0, 128), (128, 128), (256, 32))
BLOCKS = 3
ITEMS = NE * BLOCKS
LOW, HIGH = 41216, 11984

SLOPES = np.exp2(-8.0 * np.arange(1, G * H + 1) / (G * H)).astype(np.float32).reshape(G, H)


def shape_constants():
    p, f = np.arange(PART)[:, None], np.arange(PART)[None, :]
    ident = (p == f)
    pairs = (p // HD == f // HD)
    dist = np.full((PART, G, 2, PART), MASKED)
    for g in range(G):
        for kind in range(2):
            d = p - f + PART * (1 - kind)
            ok = (d >= 0) & (d <= SPAN[g]) & (d % DIL[g] == 0)
            dist[:, g, kind] = np.where(ok, d, MASKED)
    inv = np.zeros((PART, PG, 16))
    for g, w in enumerate(WINDOWS):
        inv[:, g] = 1.0 / np.minimum(np.arange(16) + 1, w)
    row = np.arange(ROWS)
    b, t, h = row // (DS * H), row // H % DS, row % H
    old = np.full((ROWS, G, PART), NEG)
    new = np.full((ROWS, HB, G, NS), NEG)
    key = np.arange(PART)
    kb, kt = np.arange(NS) // DS, np.arange(NS) % DS
    for g in range(G):
        dd = (PART + t[:, None] * (g == 0) - key[None, :]) * DIL[g]
        ok = (key[None, :] >= t[:, None]) | (g > 0)
        old[:, g] = np.where(ok, -SLOPES[g][h][:, None] * dd, NEG)
        for half in range(HB):
            dn = t[:, None] - kt[None, :]
            ok = (kb[None, :] == b[:, None] + half * BH) & ((dn >= 0) if g == 0 else (dn == 0))
            new[:, half, g] = np.where(ok, -SLOPES[g][h][:, None] * dn, NEG)
    own = (np.arange(GW)[None, :] // HD == h[:, None])
    pick = (row[:, None] // H == np.arange(BH * DS)[None, :])
    a = np.concatenate([x.reshape(PART, -1) for x in (ident, pairs, dist, inv, old, new, own, pick)], axis=1)
    real = np.stack([np.arange(PART) < n for _, n in TT], axis=1)
    m = np.concatenate([(p < f).astype(float), np.broadcast_to(f, (PART, PART)), real], axis=1)
    return a.astype(np.float32), m.astype(np.float32)


def chunk_kinds():
    return ["W"] * N_IN + ["C"] * N_CACHE + ["W"] * (N_MERGE + N_DENSE)


class Tally:

    def __init__(self, sem, layer, before=0):
        self.sem, self.layer, self.before = sem, layer, before

    def at(self, L, n):
        return self.before + L * self.layer + n


class Banks:

    def __init__(self):
        self.where, self.uses, self.turn = {}, [0] * 8, {}

    def put(self, name, pool=tuple(range(8))):
        n = self.turn.get(pool, 0)
        self.turn[pool] = n + 1
        bank = pool[n % len(pool)]
        self.where[name] = (bank, self.uses[bank])
        self.uses[bank] += 1


KPOOL, ST_BANKS, O_BANKS = (0, 1, 2, 3), (4, 5), (6, 7)


def prompt_units():
    return [(j, qt, e) for j in range(J) for qt in range(2) for e in range(2)]


UNITS = prompt_units()
K_STORES = [(g, tt) for g in range(G) for tt in range(3) if (g, tt) != (0, 0)]


def cache_tiles():
    out = [(0, b, 0, b, None) for b in range(BH)]
    for g in (1, 2):
        for b in range(BH):
            out += [(1 + BH * (g - 1) + b, t, g, b, t) for t in range(DS)]
    return out


TILES = cache_tiles()
NT = len(TILES)
MAX_AT, EXP_AT, SCALE_AT, PT_AT = 3, 6, 9, 14
PT1_AT, EX_AT = 12, 6
ROWS_AT = {5: ("ut", 0), 7: ("ut", 1), 9: ("st", 0)}


def section_pre():
    return [(("gain", 0), None)] + [(("x", tt, hf), None) for tt in range(3) for hf in range(2)]


def section_attention():
    js = [(("ssq", 0), None)]
    js += [(("u", c), None) for c in range(PG)]
    for c in range(24):
        js.append((("z", c), None))
        if c >= 2:
            js.append((("qn", c - 2), None))
        if c in ROWS_AT:
            js.append((ROWS_AT[c], None))
    js += [(("qn", 22), None), (("qn", 23), None)]
    for g in range(G):
        js += [(("zv", 4 * g + j), None) for j in range(J)]
        if g == 0:
            js += [(("yp", c), None) for c in range(PG)]
        js += [(("kt", g, tt), None) for gg, tt in K_STORES if gg == g]
        if g >= 1:
            js += [(("vt", g - 1, tt), None) for tt in range(3)]
    js += [(("vt", 2, tt), None) for tt in range(3)]
    for u in range(len(UNITS) + 3):
        if u < len(UNITS):
            js += [(("S", u, n), None) for n in range(1 + UNITS[u][1])]
        if 2 <= u < len(UNITS) + 2:
            js += [(("T", u - 2, n), None) for n in range(1 + UNITS[u - 2][1])]
        if u >= 3 and UNITS[u - 3][2] == 0:
            js.append((("O", UNITS[u - 3][0], UNITS[u - 3][1]), None))
    for half in range(HB):
        js.append((("ss", half), ST_BANKS))
        for n in range(NT):
            js.append((("kT", half, n), KPOOL))
            if half == 1 and n == PT_AT:
                js += [(("pt", 0), KPOOL), (("pn", 0), KPOOL)]
    for half in range(HB):
        js.append((("OS", half), O_BANKS))
        js += [(("pt", 1), KPOOL), (("pn", 1), KPOOL)] if half == 0 else [(("ex", 0), KPOOL)]
    for i in range(KT // 2):
        js += [((name, 2 * i + x), None) for name in ("g0", "g1") for x in range(2)]
        if i == 0:
            js.append((("ex", 1), KPOOL))
        js += [((name, 2 * i + x), None) for x in range(2) for name in ("pb", "ab")]
    js += [(("wo", c), None) for c in range(KT)]
    return js


def section_dense():
    js = [(("ssq", 1), None)]
    for i in range(FT // 2):
        js += [((name, 2 * i + x), None) for name in ("fa", "fb") for x in range(2)]
    return js + [(("fd", c), None) for c in range(KT)]


def section_moe_prep():
    js = [(("ssq", 1), None)]
    js += [(("xt", tt, hf), None) for tt in range(3) for hf in range(2)]
    js += [(("xnt", tt, hf), None) for tt in range(3) for hf in range(2)]
    js += [(("rl", tt), None) for tt in range(3)]
    return js + [(("pos", tt), None) for tt in range(3)] + [(("cnt", 0), None)]


def section_moe_item():
    js = [(("xe", n), None) for n in range(2)]
    for c in range(7):
        js += [(("eg", c), None), (("eu", c), None)]
        if c >= 1:
            js.append((("ht", c - 1), None))
    js += [(("ed", 0), None), (("ed", 1), None), (("ht", 6), None), (("gst", 0), None)]
    return js + [(("co", tt, hf), None) for tt in range(3) for hf in range(2)]


def plan(sections):
    b, out = Banks(), {}
    for name, section in sections:
        b.turn, start = {}, list(b.uses)
        b.where = {}
        for job, pool in section:
            b.put(job, pool or tuple(range(8)))
        out[name] = (dict(b.where), start, [x - y for x, y in zip(b.uses, start)])
    return out


N_GAIN = 2 * KT + PG + 2

N_IN = (IN_COLS - 2 * D) // 256
N_CACHE = 2 * HB * (1 + 2 * BH)
N_MERGE = 3 * KT // 2 + KT // 2
N_ATT = N_IN + N_CACHE + N_MERGE
N_UP, N_DOWN = 2 * (FF // 256), FT // 2
N_DENSE = N_UP + N_DOWN
N_LAYER = N_ATT + N_DENSE
N_EXPERT = 3 * (FE // 256)
C_CACHE, C_MERGE, C_UP, C_DOWN = N_IN, N_IN + N_CACHE, N_ATT, N_ATT + N_UP
assert N_LAYER % RING == 0 and N_EXPERT % MRING == 0 and N_EXPERT % MSRING == 0
N_SMALL = LAYERS * 7
R_GAP, R_CHOSEN = 9, 19
U_STORES = 1 + DB
KINDS = chunk_kinds()
C_OF = [c for c, kind in enumerate(KINDS) if kind == "W"]
W_OF = {c: w for w, c in enumerate(C_OF)}
NW_LAYER, NW_ATT = len(C_OF), sum(kind == "W" for kind in KINDS[:N_ATT])
NW = NW_LAYER + NW_ATT
W_MERGE, W_OUT, W_UP, W_DOWN = N_IN, N_IN + 3 * KT // 2, NW_ATT, NW_ATT + N_UP
DMAS = [1] * (N_IN + N_CACHE) + [1, 1, 2] * (KT // 2) + [1] * (KT // 2 + N_DENSE)
assert len(DMAS) == N_LAYER


def dmas_until(n, s):
    return sum(DMAS[c] for c in range(n) if c % RING == s)



def build(nc, io):
    plans = plan([("pre", section_pre()), ("att", section_attention()), ("dense", section_dense())])
    pre_uses = plans["pre"][2]
    layer_uses = [a + b for a, b in zip(plans["att"][2], plans["dense"][2])]
    moe_start = [p + l + a for p, l, a in zip(pre_uses, layer_uses, plans["att"][2])]
    mplans = plan([("prep", section_moe_prep()), ("item", section_moe_item())])

    ctx = ExitStack()
    with ctx:
        sem = lambda name: ctx.enter_context(nc.semaphore(name))
        low_part = ctx.enter_context(nc.sbuf_tensor("low_part", [PART, LOW], F32))
        high_part = ctx.enter_context(nc.sbuf_tensor("high_part", [PART, HIGH], F32))
        psum = ctx.enter_context(nc.psum_tensor("psum", [PART, 8, 512], F32))
        place = {"at": 0}

        def take(n, at=None):
            if at is None:
                at = place["at"]
                place["at"] = at + -(-n // 8) * 8
            return at

        def view(at, *shape):
            n = int(np.prod(shape))
            assert at + n <= LOW or LOW <= at and at + n <= LOW + HIGH, (at, n)
            flat = low_part[:, at:at + n] if at < LOW else high_part[:, at - LOW:at - LOW + n]
            if len(shape) == 1:
                return flat
            names = "abcd"[:len(shape)]
            kw = {names[i]: shape[i] for i in range(1, len(shape))}
            return flat.rearrange(f"p ({' '.join(names)}) -> p {' '.join(names)}", **kw)

        split_base = nc.sbuf_base - 4 * (LOW + HIGH)

        def split_view(name, at, *shape):
            t = nc.alloc_sbuf_tensor_at(name, [PART, int(np.prod(shape))], F32R, offset=split_base + 4 * at)
            names = "abcd"[:len(shape)]
            kw = {names[i]: shape[i] for i in range(1, len(shape))}
            return t[:, :].rearrange(f"p ({' '.join(names)}) -> p {' '.join(names)}", **kw)

        def strided(base, skip, *dims):
            return bass.AP(base.tensor, base.offset + skip, [list(base.ap[0])] + [list(d) for d in dims])

        ring_at = take(RING * CH)
        ws_at = take(SRING * 2 * CH)
        xs_at = take(2 * KT * T)
        q_at = take(12 * T)
        k_at = take(12 * T)
        v_at = take(9 * 512)
        att_at = take(J * T)
        pool_at = take(PG * T)
        p_at = take(5 * 768)
        w_pool = view(take(PG * 128), PG, 128)
        assert place["at"] <= LOW, place["at"]
        const_at = place["at"] = low_end = LOW
        ident = view(take(128), 128)
        pairs = view(take(128), 128)
        dist = view(take(G * 2 * 128), G, 2 * 128)
        inv_count = view(take(PG * 16), PG, 16)
        bias_old = view(take(G * 128), G, 128)
        bias_new = view(take(HB * G * NS), HB, G, NS)
        own_head = view(take(GW), GW)
        pick = view(take(BH * DS), BH * DS)
        const_end = place["at"]
        ones = view(take(128), 128)
        eps = view(take(1), 1)
        gains = view(take(LAYERS * N_GAIN), LAYERS, N_GAIN)
        gain = view(take(N_GAIN), N_GAIN)
        q_gain = view(take(1), 1)
        router = view(take(KT * NE), KT, NE)
        router_bias = view(take(NE), NE)
        stats = view(take(48), 48)
        k_tok = view(take(2 * 512), 2, 512)
        xT_at = take(KT * T)
        xT = view(xT_at, KT, T)
        UW = 16 + SEQ + DB * (STATE + DS)
        strips_at = take(PG * UW)
        uflat = view(strips_at, PG, UW)
        work_at = take(KT * T)
        work = view(work_at, KT, T)
        head_rms = view(take(4 * T), 4, T)
        rms = view(take(T), T)
        rstd = view(take(T), T)
        w_split = [split_view(f"w_split{i}", ws_at + 2 * CH * i, 2, CH) for i in range(SRING)]
        xn = work
        xn_split = split_view("xn_split", xs_at, 2, KT, T)
        qT, kT = view(q_at, 12, T), view(k_at, 12, T)
        v_tok = view(v_at, 3, G, 512)
        attT = view(att_at, J, T)
        poolT = view(pool_at, PG, T)
        probs = [view(p_at + 768 * i, 768) for i in range(3)]
        probsT = [view(p_at + 768 * (3 + i), 768) for i in range(2)]
        head_sq = view(work_at, 4, T)
        vT = [view(work_at + (4 - 4 * (g % 2)) * T, 4, T) for g in range(G)]
        window = [view(p_at + 768 * i, UW) for i in range(2)]
        first_mean = view(p_at + 768 * 2, 16)
        pooled = view(p_at + 768 * 3, PG, T)
        stateraw = view(pool_at, 512)
        utok = [view(p_at + 1600, 512), view(k_at + 8 * T, 512)]
        gain_raw = view(p_at, 128)
        u_new = view(p_at + 2112, PG, NS)
        q_all = view(strips_at, 12, BH, DS, H)
        q_one_at = strips_at + 12 * ROWS
        q_one = view(q_one_at, 2 * J, BH * DS, 32)
        assert 12 * ROWS + 2 * J * BH * DS * 32 <= place["at"] - strips_at
        s_probs = [view(p_at + 480 * i, G, 160) for i in range(HB)]
        sp_at = [p_at + 960, v_at]
        sp_all = [view(a, BH, DS * H) for a in sp_at]
        sp_one = [view(a + ROWS, 2, BH * DS, 32) for a in sp_at]
        sp_new = [view(a + ROWS + 1024, G, ROWS) for a in sp_at]
        o_own = view(p_at + 2496, GW)
        cacheT = [view(v_at + 1536 + 512 * i, J, 128) for i in range(3)]
        gate = [view(q_at + T * i, T) for i in range(4)]
        prod = [view(q_at + T * (4 + i), T) for i in range(4)]
        merged_split = split_view("merged_split", q_at + 8 * T, 2, KT, T)
        branch_split = split_view("branch_split", v_at, 2, 2, 4, T)
        merged = view(strips_at, KT, T)
        hid_split = split_view("hid_split", q_at, 2, FT, T)
        up_a = [view(p_at + T * i, T) for i in range(4)]
        hid = [view(p_at + T * (4 + i), T) for i in range(4)]
        x_raw = view(q_at, 3, D)
        slots = [ring_at + CH * i for i in range(MRING)]

        m = {"at": ring_at + MRING * CH}

        def mtake(n):
            at = m["at"]
            m["at"] = at + -(-n // 8) * 8
            assert m["at"] <= low_end, m["at"]
            return at

        e_split = [split_view(f"expert_split{i}", mtake(2 * CH), 2, CH) for i in range(MSRING)]
        mxn = xn
        hT_split = split_view("hT_split", xT_at, 2, ET, 128)
        x_tok = view(mtake(3 * D), 3, D)
        xn_tok = view(mtake(3 * D), 3, D)
        xe_split = split_view("xe_split", mtake(2 * D), 2, KT, 128)
        m_sig = [view(mtake(512), 512) for _ in range(2)]
        m_h = [view(mtake(512), 512) for _ in range(2)]
        ye = view(mtake(D), D)
        onehot = view(mtake(384), 3, 128)
        gated = view(mtake(384), 3, 128)
        gatedT = view(mtake(384), 3, 128)
        moe_const_at = mtake(256 + 3)
        tri, iota, real = view(moe_const_at, 128), view(moe_const_at + 128, 128), view(moe_const_at + 256, 3)
        logits = view(mtake(3 * NE), 3, NE)
        best = view(mtake(3 * 8), 3, 8)
        best_at = view(mtake(3 * 8), 3, 8).bitcast(U32)
        best_f = view(mtake(3 * 8), 3, 8)
        gap = view(mtake(3), 3, 1)
        gap_exp = view(mtake(3), 3, 1)
        gap_sum = view(mtake(3), 3, 1)
        gate1 = view(mtake(3), 3, 1)
        gate2 = view(mtake(3), 3, 1)
        hit1 = view(mtake(3 * NE), 3, NE)
        hit2 = view(mtake(3 * NE), 3, NE)
        gate_a = view(mtake(3 * NE), 3, NE)
        gate_b = view(mtake(3 * NE), 3, NE)
        chosen = view(mtake(3 * NE), 3, NE)
        place_1 = view(mtake(3 * NE), 3, NE)
        slot_of = view(mtake(3 * ITEMS), 3, ITEMS)
        gate_of = view(mtake(3 * ITEMS), 3, ITEMS)
        counts = view(mtake(NE), NE)
        flag_f = view(mtake(ITEMS), ITEMS)
        flag_sum = view(mtake(ITEMS), ITEMS)
        flags = view(mtake(2 * ITEMS), 2, ITEMS)
        flags_i = flags.bitcast(I32)

        def slot(c, ringlen=RING):
            return slots[c % ringlen]

        full = [sem(f"psum_full{b}") for b in range(8)]
        free = [sem(f"psum_free{b}") for b in range(8)]
        loaded = [sem(f"chunk_loaded{s}") for s in range(MRING)]
        raw_used = sem("cache_chunk_used")
        hi_ready = sem("chunk_high_ready")
        lo_ready = sem("chunk_low_ready")
        split_used = sem("split_chunk_used")
        small_loaded = sem("small_loaded")
        state_loaded = sem("state_loaded")
        wpool_loaded = sem("wpool_loaded")
        moe_small = sem("moe_tables_loaded")
        ones_set = sem("constants_set")
        gain_ready = Tally(sem("gain_ready"), 2)
        sq_ready = Tally(sem("squares_ready"), 16)
        rstd_ready = Tally(sem("rstd_ready"), 2)
        xn_ready = Tally(sem("xn_ready"), 16)
        win_ready = Tally(sem("window_ready"), 1 + 2 + 3 + 4)
        mean_ready = Tally(sem("mean_ready"), 2 * PG)
        hsq_ready = Tally(sem("head_squares_ready"), 24)
        hrstd_ready = Tally(sem("head_rstd_ready"), 24)
        xh_ready = Tally(sem("xn_high_ready"), 16)
        xl_ready = Tally(sem("xn_low_ready"), 16)
        zeroed = Tally(sem("sample_tiles_zeroed"), 4)
        filled = Tally(sem("queries_placed"), 16 * HB)
        bh_ready = Tally(sem("branches_high_ready"), 2)
        bl_ready = Tally(sem("branches_low_ready"), 2)
        mh_ready = Tally(sem("merged_high_ready"), KT)
        ml_ready = Tally(sem("merged_low_ready"), KT)
        hh_ready = sem("hidden_high_ready")
        hl_ready = sem("hidden_low_ready")
        eh_ready = sem("expert_high_ready")
        gains_loaded = sem("gains_loaded")
        router_loaded = sem("router_loaded")
        max_ready = Tally(sem("max_ready"), 16)
        exp_ready = Tally(sem("exp_ready"), 16)
        rden_ready = Tally(sem("rden_ready"), 16)
        p_ready = Tally(sem("probs_ready"), 16)
        scored = Tally(sem("cache_scored"), (NT - 1) * HB)
        s_max = Tally(sem("s_max_ready"), HB)
        s_exp = Tally(sem("s_exp_ready"), HB)
        s_rden = Tally(sem("s_rden_ready"), HB)
        s_p = Tally(sem("s_probs_ready"), HB)
        merged_ready = Tally(sem("merged_ready"), KT)
        u_stored = sem("u_rows_stored")
        v_stored = sem("v_rows_stored")
        k_stored = [sem(f"k_stored{i}") for i in range(2)]
        copied = sem("state_copied")
        y_stored = sem("y_stored")
        route = sem("routing_steps")
        gap_done = sem("gap_exp_ready")
        flags_ready = sem("flags_ready")
        m_hot = sem("onehot_ready")
        combined = sem("all_combined")

        class Sec:

            def __init__(self, where, base):
                self.where, self.base = where, base

            def bank(self, job):
                return self.where[job][0]

            def ps(self, job):
                return psum[:, self.bank(job), :]

            def wait_free(self, e, job):
                b, u = self.where[job]
                e.wait_ge(free[b], self.base(b) + u + 1)

            def wait_full(self, e, job):
                b, u = self.where[job]
                e.wait_ge(full[b], self.base(b) + u + 1)

            def wait_read(self, e, job):
                b, u = self.where[job]
                e.wait_ge(free[b], self.base(b) + u + 2)

            def freed(self, instruction, job):
                instruction.then_inc(free[self.where[job][0]], 1)

        def att_sec(L):
            return Sec(plans["att"][0], lambda b: L * layer_uses[b])

        pre = Sec(plans["pre"][0], lambda b: 0)
        dense_sec = Sec(plans["dense"][0], lambda b: 0)
        prep = Sec(mplans["prep"][0], lambda b: moe_start[b])

        def item_sec(seq):
            per = mplans["item"][2]
            return Sec(mplans["item"][0], lambda b: moe_start[b] + seq * per[b])

        def item_before(seq):
            per = mplans["item"][2]
            return Sec(mplans["item"][0], lambda b: moe_start[b] + seq * per[b] - per[b])

        def wait_chunk(e, L, c):
            e.wait_ge(loaded[c % RING], 16 * (L * dmas_until(N_LAYER, c % RING) + dmas_until(c + 1, c % RING)))

        def wait_moe_chunk(e, seq, c):
            s = c % MRING
            before = dmas_until(N_LAYER, s) + dmas_until(N_ATT, s) if s < RING else 0
            e.wait_ge(loaded[s], 16 * (before + seq * (N_EXPERT // MRING) + c // MRING + 1))

        def wait_cache_scored(e, L, S, m):
            if m >= 0:
                half, n = m // NT, m % NT
                if n == NT - 1:
                    S.wait_full(e, ("ss", half))
                else:
                    e.wait_ge(scored.sem, scored.at(L, half * (NT - 1) + n + 1))

        def through_items(e, item, start=0):
            with e.Fori(start, ITEMS) as i:
                flag = e.value_load(flags_i[0:1, 0, bass.ds(i, 1)], min_val=0, max_val=1)
                seq = e.value_load(flags_i[0:1, 1, bass.ds(i, 1)], min_val=0, max_val=ITEMS - 1)
                with e.If(flag > 0):
                    item(i, seq)

        block = ctx.enter_context(nc.Block())

        @block.sync
        def _(e):
            for tt, (a, n) in enumerate(TT):
                src = io["x_prompt"][0, a:a + n, :] if tt < 2 else io["x_sample"].rearrange("b t d -> (b t) d")
                e.dma_start(x_raw[0:n, tt, :], src).then_inc(small_loaded, 16)
            e.dma_start(view(const_at, const_end - const_at), io["const_a"]).then_inc(small_loaded, 16)

            def send(L, c, parts):
                assert len(parts) == DMAS[c]
                before = L * N_LAYER + c - RING
                if before >= 0:
                    L0, c0 = divmod(before, N_LAYER)
                    if KINDS[c0] == "W":
                        e.wait_ge(lo_ready, L0 * NW_LAYER + W_OF[c0] + 1)
                    else:
                        e.wait_ge(raw_used, L0 * N_CACHE + c0 - C_CACHE + 1)
                for dst, src in parts:
                    e.dma_start(dst, src).then_inc(loaded[c % RING], 16)

            def columns(w, a):
                return w.rearrange("(k p) n -> p k n", p=PART)[:, :, a:a + 256]

            def send_attention(L):
                for c in range(N_IN):
                    send(L, c, [(view(slot(c), KT, 256), columns(io["w_in"][L], 256 * c))])
                c = C_CACHE
                for kv in range(2):
                    for half in range(HB):
                        b0 = half * BH
                        send(L, c, [(view(slot(c), BH, 512),
                                     io["cache_kv_g0"][L, b0:b0 + BH, :, kv].rearrange("b m h d -> m b (h d)"))])
                        c += 1
                        for g in (1, 2):
                            for b in range(b0, b0 + BH):
                                send(L, c, [(view(slot(c), DS, 512), io[f"cache_kv_g{g}"][L, b].rearrange(
                                    "(m r) v h d -> m r v (h d)", r=DIL[g])[:, 0:DS, kv])])
                                c += 1
                for i in range(KT // 2):
                    for b in range(2):
                        send(L, c, [(view(slot(c), KT, 256), columns(io["w_in"][L], IN_COLS - 2 * D + b * D + 256 * i))])
                        c += 1
                    dst = view(slot(c), 2, 4, 256)
                    send(L, c, [(dst[:, b], columns(io[name][L], 256 * i))
                                for b, name in enumerate(("w_branch_pool", "w_branch_attn"))])
                    c += 1
                for i in range(KT // 2):
                    send(L, c, [(view(slot(c), KT, 256), columns(io["w_out"][L], 256 * i))])
                    c += 1
                assert c == N_ATT

            def send_dense():
                for i in range(FT // 2):
                    for b, name in enumerate(("w1_dense", "w3_dense")):
                        c = C_UP + 2 * i + b
                        send(0, c, [(view(slot(c), KT, 256), columns(io[name][0], 256 * i))])
                w2 = io["w2_dense"][0].rearrange("(f p) n -> p f n", p=PART)
                for i in range(N_DOWN):
                    send(0, C_DOWN + i, [(view(slot(C_DOWN + i), 2, D), w2[:, 2 * i:2 * i + 2, :])])

            send_attention(0)
            send_dense()
            send_attention(1)

            e.wait_ge(lo_ready, NW)
            e.wait_ge(split_used, NW)
            e.wait_ge(v_stored, LAYERS * 16 * len(K_STORES))
            e.wait_ge(u_stored, LAYERS * 16 * U_STORES)
            e.wait_ge(copied, LAYERS * 16)
            for i in range(2):
                e.wait_ge(k_stored[i], LAYERS * 16 * (len(K_STORES) // 2))
            e.dma_start(view(moe_const_at, 259), io["const_m"]).then_inc(moe_small, 16)

            def send_item(i, seq):
                ex = i // BLOCKS
                for c in range(N_EXPERT):
                    e.wait_ge(lo_ready, NW + seq * N_EXPERT + c - MRING + 1)
                    if c < 28:
                        name, a = ("we_gate", "we_up")[c // 2 % 2], 512 * (c // 4) + 256 * (c % 2)
                        dst, src = view(slot(c, MRING), KT, 256), columns(io[name][0, ex], a)
                    else:
                        dst = view(slot(c, MRING), 2, D)
                        src = io["we_down"][0, ex].rearrange("(f p) n -> p f n", p=PART)[:, 2 * (c - 28):2 * (c - 27), :]
                    e.dma_start(dst, src).then_inc(loaded[c % MRING], 16)

            send_item(0, 0)
            e.wait_ge(flags_ready, 1)
            through_items(e, send_item, 1)
            e.wait_ge(combined, 1)
            for tt, (a, n) in enumerate(TT):
                dst = io["y_prompt"][0, a:a + n, :] if tt < 2 else io["y_sample"].rearrange("b t d -> (b t) d")
                e.dma_start(dst, x_tok[0:n, tt, :]).then_inc(y_stored, 16)
            e.wait_ge(y_stored, 48)

        @block.tensor
        def _(e):
            done = []

            def signal(r, inc):
                if inc is not None:
                    r.then_inc(inc, 1)
                elif done:
                    r.then_inc(done.pop(0), 1)

            def mm(out, lhsT, rhs, start, stop, inc=None, mixed=False):
                signal(e.matmul(out, lhsT, rhs, start=start, stop=stop, skip_group_check=mixed), inc)

            def mm3(out, lhsT, rhs, start, stop, inc=None):
                for n, (a, b) in enumerate(((0, 0), (0, 1), (1, 0))):
                    mm(out, lhsT[a], rhs[b], start and n == 0, stop and n == 2, inc if n == 2 else None)

            def turn(out, in_, inc=None):
                signal(e.transpose(out, in_, ident[0:in_.shape[0], 0:in_.shape[0]]), inc)

            def ssq(L, S, i):
                S.wait_free(e, ("ssq", i))
                for k in range(KT):
                    e.wait_ge(sq_ready.sem, sq_ready.at(L, 8 * i + k + 1))
                    mm(S.ps(("ssq", i))[:, 0:T], ones, work[:, k, :], k == 0, k == KT - 1,
                       full[S.bank(("ssq", i))] if k == KT - 1 else None)

            def chunk(L, w):
                e.wait_ge(lo_ready, L * NW_LAYER + w + 1)
                return w_split[(L * NW_LAYER + w) % SRING]

            def project(S, job, w, rhs, n=KT):
                S.wait_free(e, job)
                for k in range(n):
                    mm3(S.ps(job)[:, 0:T], [w(0, k), w(1, k)], [rhs[:, 0, k, :], rhs[:, 1, k, :]], k == 0, k == n - 1,
                        full[S.bank(job)] if k == n - 1 else None)

            e.wait_ge(small_loaded, 64)
            for tt, (_, n) in enumerate(TT):
                for hf in range(2):
                    job = ("x", tt, hf)
                    pre.wait_free(e, job)
                    for i in range(4):
                        turn(pre.ps(job)[:, i * 128:i * 128 + n], x_raw[0:n, tt, (4 * hf + i) * 128:(4 * hf + i + 1) * 128],
                             full[pre.bank(job)] if i == 3 else None)
            e.wait_ge(gains_loaded, 16 * N_SMALL)
            pre.wait_free(e, ("gain", 0))
            turn(pre.ps(("gain", 0))[:, 0:LAYERS * N_GAIN], gain_raw[0:LAYERS * N_GAIN, :], full[pre.bank(("gain", 0))])
            e.wait_ge(ones_set, 3)

            def attention(L):
                S = att_sec(L)
                ssq(L, S, 0)

                def column_tile(job, c):
                    w = chunk(L, c // 2).rearrange("p a (k n) -> p a k n", k=KT)
                    project(S, job, lambda a, k: w[:, a, k, 128 * (c % 2):128 * (c % 2 + 1)], xn_split)
                    if c % 2 == 1:
                        done.append(split_used)

                def head_norm(c):
                    S.wait_free(e, ("qn", c))
                    e.wait_ge(hsq_ready.sem, hsq_ready.at(L, c + 1))
                    mm(S.ps(("qn", c))[:, 0:T], pairs, head_sq[:, c % 4, :], True, True, full[S.bank(("qn", c))])

                def turn_rows(job, tile, a, n, count=4):
                    S.wait_free(e, job)
                    for i in range(count):
                        turn(S.ps(job)[0:n, 128 * i:128 * (i + 1)], tile(i)[:, a:a + n],
                             full[S.bank(job)] if i == count - 1 else None)

                e.wait_ge(xl_ready.sem, xl_ready.at(L, KT))
                for c in range(PG):
                    column_tile(("u", c), c)
                for c in range(24):
                    column_tile(("z", c), PG + c)
                    if c >= 2:
                        head_norm(c - 2)
                    if c == 5:
                        S.wait_read(e, ("u", PG - 1))
                        turn_rows(("ut", 0), lambda i: uflat[:, i, 16:16 + SEQ], SEQ - STATE, STATE)
                    if c == 7:
                        turn_rows(("ut", 1), lambda i: u_new[:, i, :], 0, NS)
                    if c == 9:
                        S.wait_free(e, ("st", 0))
                        e.wait_ge(state_loaded, 16 * (L + 1))
                        for i in range(PG):
                            turn(S.ps(("st", 0))[:, 120 * i:120 * (i + 1)], stateraw[0:120, 128 * i:128 * (i + 1)],
                                 full[S.bank(("st", 0))] if i == PG - 1 else None)
                head_norm(22)
                head_norm(23)

                def value_rows(g):
                    S.wait_read(e, ("zv", 4 * g + 3))
                    for tt, (a, n) in enumerate(TT):
                        turn_rows(("vt", g, tt), lambda i: vT[g][:, i, :], a, n)

                for g in range(G):
                    for j in range(J):
                        column_tile(("zv", 4 * g + j), PG + 24 + 4 * g + j)
                    if g == 0:
                        e.wait_ge(wpool_loaded, 16 * (L + 1))
                        for c in range(PG):
                            S.wait_free(e, ("yp", c))
                            e.wait_ge(mean_ready.sem, mean_ready.at(L, 2 * c + 2))
                            mm(S.ps(("yp", c))[:, 0:T], w_pool[:, c, :], pooled[:, c, :], True, True,
                               full[S.bank(("yp", c))])
                    S.wait_read(e, ("z", 12 + 4 * g + 3))
                    for gg, tt in K_STORES:
                        if gg == g:
                            turn_rows(("kt", g, tt), lambda i: kT[:, 4 * g + i, :], *TT[tt])
                    if g >= 1:
                        value_rows(g - 1)
                value_rows(G - 1)

                def scores(u):
                    j, qt, he = UNITS[u]
                    p = slice(64 * he, 64 * he + 64)
                    w = 128 * (qt + 1)
                    for n in range(1 + qt):
                        S.wait_free(e, ("S", u, n))
                    for g in range(G):
                        job = ("S", u, 1 if qt and g == 2 else 0)
                        last = g == 2 or (qt and g == 1)
                        at = 0 if qt and g == 2 else g * w
                        mm(S.ps(job)[:, at:at + w], qT[p, 4 * g + j, 128 * qt:128 * qt + 128],
                           kT[p, 4 * g + j, 0:w], True, True, full[S.bank(job)] if last else None)

                def turn_probs(u):
                    j, qt, he = UNITS[u]
                    e.wait_ge(p_ready.sem, p_ready.at(L, u + 1))
                    n = G * (qt + 1)
                    for i in range(n):
                        job = ("T", u, i // 4)
                        if i % 4 == 0:
                            S.wait_free(e, job)
                        turn(S.ps(job)[:, 128 * (i % 4):128 * (i % 4 + 1)], probs[u % 3][:, 128 * i:128 * (i + 1)],
                             full[S.bank(job)] if i == n - 1 or i % 4 == 3 else None)

                def values(u):
                    j, qt, he = UNITS[u]
                    job = ("O", j, qt)
                    if he == 0:
                        S.wait_free(e, job)
                    for n in range(1 + qt):
                        S.wait_read(e, ("T", u, n))
                    n = G * (qt + 1)
                    for i in range(n):
                        g, kt = i // (qt + 1), i % (qt + 1)
                        h = 2 * j + he
                        mm(S.ps(job)[64 * he:64 * he + 64, 0:128], v_tok[:, kt, g, 64 * h:64 * h + 64],
                           probsT[u % 2][:, 128 * i:128 * (i + 1)], i == 0, i == n - 1,
                           full[S.bank(job)] if he == 1 and i == n - 1 else None)

                S.wait_read(e, ("vt", 2, 2))
                for u in range(len(UNITS) + 3):
                    if u < len(UNITS):
                        scores(u)
                    if 2 <= u < len(UNITS) + 2:
                        turn_probs(u - 2)
                    if u >= 3:
                        values(u - 3)

                def cache_tile(first_chunk, half, n):
                    where, i, g, b, t = TILES[n]
                    c = first_chunk + (1 + 2 * BH) * half + where
                    if n == 0 or TILES[n - 1][0] != where:
                        wait_chunk(e, L, c)
                    return view(slot(c) + 512 * i, 512)

                def release(n):
                    if n == NT - 1 or TILES[n + 1][0] != TILES[n][0]:
                        done.append(raw_used)

                def turn_cache(half, n):
                    job = ("kT", half, n)
                    tile = cache_tile(C_CACHE, half, n)
                    S.wait_free(e, job)
                    for j in range(J):
                        turn(S.ps(job)[:, 128 * j:128 * (j + 1)], tile[:, 128 * j:128 * (j + 1)],
                             full[S.bank(job)] if j == J - 1 else None)
                    release(n)

                def score_new(half):
                    job = ("ss", half)
                    S.wait_free(e, job)
                    e.wait_ge(filled.sem, filled.at(L, 16 * (half + 1)))
                    for g in range(G):
                        for j in range(J):
                            mm(S.ps(job)[:, 160 * g + 128:160 * (g + 1)],
                               q_all[:, 4 * g + j].rearrange("p b t h -> p (b t h)"), kT[:, 4 * g + j, SEQ:T],
                               g == 0 and j == 0, False, mixed=True)

                def score_cache(m):
                    half, n = m // NT, m % NT
                    _, _, g, b, t = TILES[n]
                    job = ("ss", half)
                    S.wait_read(e, ("kT", half, n))
                    for j in range(J):
                        inc = None
                        if j == J - 1:
                            inc = full[S.bank(job)] if n == NT - 1 else scored.sem
                        q = (q_all[:, j, b].rearrange("p t h -> p (t h)") if g == 0
                             else q_one[:, 4 * (g - 1) + j, DS * b + t, :])
                        mm(S.ps(job)[32 * b:32 * b + 32, 160 * g:160 * g + 128], q, cacheT[m % 3][:, j, :],
                           False, n == NT - 1 and j == J - 1, inc, mixed=True)

                def turn_s_probs(half):
                    e.wait_ge(s_p.sem, s_p.at(L, half + 1))
                    for name, lo, n in (("pt", 0, 128), ("pn", 128, NS)):
                        job = (name, half)
                        S.wait_free(e, job)
                        for g in range(G):
                            turn(S.ps(job)[0:n, 128 * g:128 * (g + 1)], s_probs[half][:, g, lo:lo + n],
                                 full[S.bank(job)] if g == G - 1 else None)

                LAG = 2
                score_new(0)
                for m in range(HB * NT + LAG):
                    if m < HB * NT:
                        turn_cache(m // NT, m % NT)
                    if m == NT + LAG:
                        score_new(1)
                    if m >= LAG:
                        score_cache(m - LAG)
                    if m == NT + PT_AT:
                        turn_s_probs(0)

                def gather_heads(half):
                    job = ("ex", half)
                    S.wait_free(e, job)
                    S.wait_read(e, ("OS", half))
                    for j in range(J):
                        mm(S.ps(job)[:, 16 * j:16 * (j + 1)], o_own[:, 128 * j:128 * (j + 1)], pick, True, True,
                           full[S.bank(job)] if j == J - 1 else None)

                for half in range(HB):
                    job = ("OS", half)
                    S.wait_free(e, job)
                    S.wait_read(e, ("pt", half))
                    S.wait_read(e, ("pn", half))
                    for g in range(G):
                        mm(S.ps(job), sp_new[half][0:NS, g, :], v_tok[0:NS, 2, g, :], g == 0, False, mixed=True)
                    for n in range(NT):
                        _, _, g, b, t = TILES[n]
                        tile = cache_tile(C_CACHE + 2 * (1 + 2 * BH), half, n)
                        p = sp_all[half][:, b, :] if g == 0 else sp_one[half][:, g - 1, DS * b + t, :]
                        last = n == NT - 1
                        mm(S.ps(job)[32 * b:32 * b + 32], p, tile, False, last, full[S.bank(job)] if last else None, mixed=True)
                        release(n)
                        if half == 0 and n == PT1_AT:
                            turn_s_probs(1)
                        if half == 1 and n == EX_AT:
                            gather_heads(0)

                for i in range(KT // 2):
                    for b in range(2):
                        w = chunk(L, W_MERGE + 3 * i + b).rearrange("p a (k n) -> p a k n", k=KT)
                        for x in range(2):
                            project(S, (f"g{b}", 2 * i + x), lambda a, k: w[:, a, k, 128 * x:128 * (x + 1)], xn_split)
                        done.append(split_used)
                    if i == 0:
                        gather_heads(1)
                        e.wait_ge(bl_ready.sem, bl_ready.at(L, 2))
                    w = chunk(L, W_MERGE + 3 * i + 2).rearrange("p a (b k n) -> p a b k n", b=2, k=4)
                    for x in range(2):
                        for b in range(2):
                            project(S, (("pb", "ab")[b], 2 * i + x), lambda a, k: w[:, a, b, k, 128 * x:128 * (x + 1)],
                                    branch_split[:, b], 4)
                    done.append(split_used)
                e.wait_ge(ml_ready.sem, ml_ready.at(L, KT))
                for c in range(KT):
                    w = chunk(L, W_OUT + c // 2).rearrange("p a (k n) -> p a k n", k=KT)
                    project(S, ("wo", c), lambda a, k: w[:, a, k, 128 * (c % 2):128 * (c % 2 + 1)], merged_split)
                    if c % 2 == 1:
                        done.append(split_used)

            def ffn():
                S = dense_sec
                ssq(0, S, 1)
                e.wait_ge(xl_ready.sem, xl_ready.at(0, 2 * KT))
                for i in range(FT // 2):
                    for b in range(2):
                        w = chunk(0, W_UP + 2 * i + b).rearrange("p a (k n) -> p a k n", k=KT)
                        for x in range(2):
                            project(S, (("fa", "fb")[b], 2 * i + x), lambda a, k: w[:, a, k, 128 * x:128 * (x + 1)], xn_split)
                        done.append(split_used)
                for f in range(FT):
                    w = chunk(0, W_DOWN + f // 2).rearrange("p a (f n) -> p a f n", f=2)
                    e.wait_ge(hl_ready, f + 1)
                    for n in range(KT):
                        job = ("fd", n)
                        if f == 0:
                            S.wait_free(e, job)
                        mm3(S.ps(job)[:, 0:T], [w[:, a, f % 2, 128 * n:128 * (n + 1)] for a in range(2)],
                            [hid_split[:, a, f, :] for a in range(2)], f == 0, f == FT - 1,
                            full[S.bank(job)] if f == FT - 1 else None)
                    if f % 2 == 1:
                        done.append(split_used)

            attention(0)
            ffn()
            attention(1)

            P = prep
            ssq(1, P, 1)
            assert not done
            for name, src in (("xt", xT), ("xnt", mxn)):
                for tt, (a, n) in enumerate(TT):
                    for hf in range(2):
                        job = (name, tt, hf)
                        P.wait_free(e, job)
                        if name == "xnt" and tt == 0:
                            e.wait_ge(xn_ready.sem, xn_ready.at(1, 8 + 4 * (hf + 1)))
                        for i in range(4):
                            turn(P.ps(job)[0:n, 128 * i:128 * (i + 1)], src[:, 4 * hf + i, a:a + n],
                                 full[P.bank(job)] if i == 3 else None)
            e.wait_ge(router_loaded, 32)
            for tt, (a, n) in enumerate(TT):
                job = ("rl", tt)
                P.wait_free(e, job)
                for k in range(KT):
                    mm(P.ps(job)[0:n, 0:NE], mxn[:, k, a:a + n], router[:, k, :], k == 0, False)
                mm(P.ps(job)[0:n, 0:NE], ones[0:1, 0:n], router_bias[0:1, :], False, True, full[P.bank(job)])
            e.wait_ge(route, R_CHOSEN)
            e.wait_ge(moe_small, 16)
            for tt in range(3):
                job = ("pos", tt)
                P.wait_free(e, job)
                for t2 in range(tt):
                    mm(P.ps(job)[:, 0:NE], ones, chosen[:, t2, :], t2 == 0, False)
                mm(P.ps(job)[:, 0:NE], tri, chosen[:, tt, :], tt == 0, True, full[P.bank(job)])
            P.wait_free(e, ("cnt", 0))
            for tt in range(3):
                mm(P.ps(("cnt", 0))[:, 0:NE], ones, chosen[:, tt, :], tt == 0, tt == 2,
                   full[P.bank(("cnt", 0))] if tt == 2 else None)
            P.wait_read(e, ("xnt", 2, 1))
            e.wait_ge(flags_ready, 1)

            def item(i, seq):
                I = item_sec(seq)
                e.wait_ge(m_hot, 6 * seq + 6)
                for n in range(2):
                    job = ("xe", n)
                    I.wait_free(e, job)
                    for k in range(4):
                        for tt, (_, nt) in enumerate(TT):
                            mm(I.ps(job)[:, 128 * k:128 * (k + 1)], xn_tok[0:nt, tt, 128 * (4 * n + k):128 * (4 * n + k + 1)],
                               onehot[0:nt, tt, :], tt == 0, tt == 2, full[I.bank(job)] if k == 3 and tt == 2 else None)

                def expert_chunk(v):
                    e.wait_ge(lo_ready, NW + seq * N_EXPERT + v + 1)
                    return e_split[v % MSRING]

                def turn_hidden(c):
                    job = ("ht", c)
                    I.wait_free(e, job)
                    I.wait_read(e, ("eu", c))
                    for i in range(4):
                        turn(I.ps(job)[:, 128 * i:128 * (i + 1)], m_h[c % 2][:, 128 * i:128 * (i + 1)],
                             full[I.bank(job)] if i == 3 else None)

                I.wait_read(e, ("xe", 0))
                I.wait_read(e, ("xe", 1))
                for c in range(7):
                    for b in range(2):
                        job = (("eg", "eu")[b], c)
                        I.wait_free(e, job)
                        for x in range(2):
                            w = expert_chunk(4 * c + 2 * b + x).rearrange("p a (k n) -> p a k n", k=KT)
                            for k in range(KT):
                                mm3(I.ps(job)[:, 256 * x:256 * (x + 1)], [xe_split[:, a, k, :] for a in range(2)],
                                    [w[:, a, k, :] for a in range(2)], k == 0, k == KT - 1,
                                    full[I.bank(job)] if x == 1 and k == KT - 1 else None)
                            done.append(split_used)
                    if c >= 1:
                        turn_hidden(c - 1)
                for hf in range(2):
                    I.wait_free(e, ("ed", hf))
                for f in range(ET):
                    if f % 2 == 0:
                        w = expert_chunk(28 + f // 2).rearrange("p a (f n) -> p a f n", f=2)
                    if f % 4 == 0:
                        I.wait_read(e, ("ht", f // 4))
                    for hf in range(2):
                        job = ("ed", hf)
                        mm3(I.ps(job), [hT_split[:, a, f, :] for a in range(2)],
                            [w[:, a, f % 2, 512 * hf:512 * (hf + 1)] for a in range(2)], f == 0, f == ET - 1,
                            full[I.bank(job)] if f == ET - 1 else None)
                    if f % 2 == 1:
                        done.append(split_used)
                    if f == 3:
                        turn_hidden(6)
                job = ("gst", 0)
                I.wait_free(e, job)
                for tt, (_, nt) in enumerate(TT):
                    turn(I.ps(job)[:, 128 * tt:128 * tt + nt], gated[0:nt, tt, :], full[I.bank(job)] if tt == 2 else None)
                I.wait_read(e, ("gst", 0))
                I.wait_read(e, ("ed", 0))
                I.wait_read(e, ("ed", 1))
                for tt, (_, nt) in enumerate(TT):
                    for hf in range(2):
                        job = ("co", tt, hf)
                        I.wait_free(e, job)
                        mm(I.ps(job)[0:nt], gatedT[:, tt, 0:nt], ye[:, 512 * hf:512 * (hf + 1)], True, True,
                           full[I.bank(job)])
                assert not done

            through_items(e, item)

        @block.scalar
        def _(e):
            def copy(S, job, out, in_):
                S.wait_full(e, job)
                S.freed(e.activation(out, in_, ACT.Copy), job)

            def norm(L, S, i, w=None):
                for k in range(KT):
                    e.activation(work[:, k, :], xT[:, k, :], ACT.Square).then_inc(sq_ready.sem, 1)
                if w is not None:
                    split_high(L, w)
                S.wait_full(e, ("ssq", i))
                S.freed(e.activation(rms, S.ps(("ssq", i))[:, 0:T], ACT.Sqrt, bias=eps[:, 0:1], scale=1.0 / D), ("ssq", i))

            def split_high(L, w):
                c, gw = C_OF[w], L * NW_LAYER + w
                wait_chunk(e, L, c)
                if gw >= SRING:
                    e.wait_ge(split_used, gw - SRING + 1)
                e.activation(w_split[gw % SRING][:, 0, :], view(slot(c), CH), ACT.Copy).then_inc(hi_ready, 1)

            def split_norm(L, i):
                for k in range(KT):
                    e.wait_ge(xn_ready.sem, xn_ready.at(L, 8 * i + k + 1))
                    e.activation(xn_split[:, 0, k, :], xn[:, k, :], ACT.Copy).then_inc(xh_ready.sem, 1)

            at = 0
            for L in range(LAYERS):
                rows = [io[n][L].rearrange("(k p) -> k p", p=PART) for n in ("norm_attn", "norm_ffn", "pool_scale")]
                for src in rows:
                    n = src.shape[0]
                    e.dma_start(gain_raw[at:at + n, :], src).then_inc(gains_loaded, 16)
                    at += n
                for name in ("q_norm", "k_norm"):
                    for he in range(2):
                        e.dma_start(gain_raw[at:at + 1, 64 * he:64 * he + 64], io[name][L:L + 1, :]).then_inc(gains_loaded, 16)
                    at += 1
            e.dma_start(router, io["router_w"][0].rearrange("(k p) n -> p k n", p=PART)).then_inc(router_loaded, 16)
            e.dma_start(router_bias[0:1, :], io["router_b"]).then_inc(router_loaded, 16)

            e.wait_ge(ones_set, 3)
            pre.wait_read(e, ("x", 2, 1))

            def attention(L):
                S = att_sec(L)
                if L == 0:
                    split_high(0, 0)
                norm(L, S, 0, 1)
                split_norm(L, 0)

                for w in range(2, N_IN):
                    if w + 1 < N_IN:
                        if w == 2:
                            split_high(L, 2)
                        split_high(L, w + 1)
                    for c in (2 * w - 4, 2 * w - 3):
                        if c < 24:
                            S.wait_full(e, ("z", c))
                            e.activation(head_sq[:, c % 4, :], S.ps(("z", c))[:, 0:T], ACT.Square).then_inc(hsq_ready.sem, 1)
                        if 2 <= c < 26:
                            v = c - 2
                            S.wait_full(e, ("qn", v))
                            if v >= 4:
                                S.wait_read(e, ("z", v - 4))
                            S.freed(e.activation(head_rms[:, v % 4, :], S.ps(("qn", v))[:, 0:T], ACT.Sqrt,
                                                 bias=eps[:, 0:1], scale=1.0 / HD), ("qn", v))
                        if c >= 24:
                            v = c - 24
                            copy(S, ("zv", v), vT[v // 4][:, v % 4, :], S.ps(("zv", v))[:, 0:T])

                for u in range(len(UNITS) + 2):
                    if u >= 2:
                        v = u - 2
                        for n in range(1 + UNITS[v][1]):
                            w = min(512, 128 * G * (UNITS[v][1] + 1) - 512 * n)
                            copy(S, ("T", v, n), probsT[v % 2][:, 512 * n:512 * n + w], S.ps(("T", v, n))[:, 0:w])
                    if u < len(UNITS):
                        w = 128 * G * (UNITS[u][1] + 1)
                        e.wait_ge(max_ready.sem, max_ready.at(L, u + 1))
                        e.activation(probs[u % 3][:, 0:w], probs[u % 3][:, 0:w], ACT.Exp, bias=stats[:, u:u + 1],
                                     accum_out=stats[:, 16 + u:17 + u]).then_inc(exp_ready.sem, 1)

                e.wait_ge(v_stored, 16 * len(K_STORES) * (L + 1))
                for m in range(HB * NT):
                    if m % 2 == 0:
                        wait_cache_scored(e, L, S, m - 3)
                        copy(S, ("kT", m // NT, m % NT), cacheT[m % 3], S.ps(("kT", m // NT, m % NT))
                             .rearrange("p (j m) -> p j m", j=J))
                    if m == NT + EXP_AT:
                        sample_exp(e, L, 0)
                    if m == NT + PT_AT + 2:
                        place_probs(e, L, S, 0)
                sample_exp(e, L, 1)
                place_probs(e, L, S, 1)
                split_high(L, W_MERGE)
                split_high(L, W_MERGE + 1)

                for i in range(KT // 2):
                    for b in range(2):
                        w = W_MERGE + 3 * i + b
                        if w > W_MERGE:
                            split_high(L, w + 1)
                        for x in range(2):
                            c = 2 * i + x
                            if c >= 2:
                                S.wait_read(e, (("pb", "ab")[b], c - 2))
                            S.wait_full(e, (f"g{b}", c))
                            S.freed(e.activation(gate[(2 * c + b) % 4], S.ps((f"g{b}", c))[:, 0:T], ACT.Sigmoid), (f"g{b}", c))
                    if i == 0:
                        S.wait_read(e, ("yp", PG - 1))
                        e.activation(branch_split[:, 0, 0], poolT, ACT.Copy).then_inc(bh_ready.sem, 1)
                        S.wait_read(e, ("ex", 1))
                        e.activation(branch_split[:, 1, 0], attT, ACT.Copy).then_inc(bh_ready.sem, 1)
                    split_high(L, W_MERGE + 3 * i + 3)
                    for c in ((2 * i - 2, 2 * i - 1) if i else ()):
                        merge_high(e, L, c)
                for c in range(KT - 2, KT):
                    merge_high(e, L, c)
                for w in range(W_OUT + 1, NW_ATT + (L == 0)):
                    split_high(L, w)
                for c in range(KT):
                    S.wait_read(e, ("wo", c))

            def merge_high(e, L, c):
                e.wait_ge(merged_ready.sem, merged_ready.at(L, c + 1))
                e.activation(merged_split[:, 0, c, :], merged[:, c, :], ACT.Copy).then_inc(mh_ready.sem, 1)

            def sample_exp(e, L, half):
                e.wait_ge(s_max.sem, s_max.at(L, half + 1))
                flat = s_probs[half].rearrange("p g k -> p (g k)")
                e.activation(flat, flat, ACT.Exp, bias=stats[:, half:half + 1],
                             accum_out=stats[:, 16 + half:17 + half]).then_inc(s_exp.sem, 1)

            def place_probs(e, L, S, half):
                job = ("pt", half)
                S.wait_full(e, job)
                e.wait_ge(zeroed.sem, zeroed.at(L, 4))
                ps = S.ps(job)
                e.activation(sp_all[half].rearrange("p b r -> p (b r)"), ps[:, 0:128], ACT.Copy)
                for g in (1, 2):
                    one = view(sp_at[half] + ROWS + 512 * (g - 1), 512)
                    r = e.activation(strided(one, 0, (128, BH), (32 + H, DS), (1, H)),
                                     ps[:, 128 * g:128 * (g + 1)].rearrange("p (b t h) -> p b t h", b=BH, t=DS), ACT.Copy)
                S.freed(r, job)

            def ffn():
                S = dense_sec
                norm(0, S, 1, W_UP + 1)
                split_norm(0, 1)

                def hidden_high(f):
                    S.wait_read(e, ("fb", f))
                    e.activation(hid_split[:, 0, f, :], hid[f % 4], ACT.Copy).then_inc(hh_ready, 1)

                for i in range(FT // 2):
                    if i >= 1:
                        split_high(0, W_UP + 2 * i + 1)
                        hidden_high(2 * i - 2)
                        hidden_high(2 * i - 1)
                    for f in (2 * i, 2 * i + 1):
                        if f >= 4:
                            S.wait_read(e, ("fb", f - 4))
                        S.wait_full(e, ("fa", f))
                        S.freed(e.activation(up_a[f % 4], S.ps(("fa", f))[:, 0:T], ACT.Silu), ("fa", f))
                    split_high(0, W_UP + 2 * i + 2)
                split_high(0, W_DOWN + 1)
                hidden_high(FT - 2)
                hidden_high(FT - 1)
                for w in range(W_DOWN + 2, NW_LAYER):
                    split_high(0, w)
                split_high(1, 0)
                for c in range(KT):
                    S.wait_read(e, ("fd", c))

            attention(0)
            ffn()
            attention(1)

            P = prep
            norm(1, P, 1)
            for tt, (_, n) in enumerate(TT):
                for hf in range(2):
                    job = ("xnt", tt, hf)
                    copy(P, job, xn_tok[0:n, tt, 512 * hf:512 * (hf + 1)], P.ps(job)[0:n])
            e.wait_ge(route, R_GAP)
            e.activation(gap_exp[:, :, 0], gap[:, :, 0], ACT.Exp).then_inc(gap_done, 1)
            e.wait_ge(flags_ready, 1)

            e.wait_ge(split_used, NW)

            def item(i, seq):
                I = item_sec(seq)

                def expert_high(v):
                    if v >= N_EXPERT:
                        return
                    wait_moe_chunk(e, seq, v)
                    e.wait_ge(split_used, NW + seq * N_EXPERT + v - MSRING + 1)
                    e.activation(e_split[v % MSRING][:, 0, :], view(slot(v, MRING), CH), ACT.Copy).then_inc(hi_ready, 1)

                def high(job, out):
                    I.wait_full(e, job)
                    e.activation(out, I.ps(job).rearrange("p (k s) -> p k s", k=4), ACT.Copy).then_inc(eh_ready, 1)

                expert_high(0)
                expert_high(1)
                for n in range(2):
                    high(("xe", n), xe_split[:, 0, 4 * n:4 * n + 4, :])
                for c in range(7):
                    expert_high(4 * c + 2)
                    expert_high(4 * c + 3)
                    if c >= 2:
                        I.wait_read(e, ("eu", c - 2))
                    I.wait_full(e, ("eg", c))
                    I.freed(e.activation(m_sig[c % 2], I.ps(("eg", c)), ACT.Silu), ("eg", c))
                    expert_high(4 * c + 4)
                    expert_high(4 * c + 5)
                    if c >= 1:
                        high(("ht", c - 1), hT_split[:, 0, 4 * c - 4:4 * c, :])
                for v in range(28, N_EXPERT):
                    expert_high(v + 2)
                    if v == 29:
                        high(("ht", 6), hT_split[:, 0, 24:28, :])
                copy(I, ("ed", 0), ye[:, 0:512], I.ps(("ed", 0)))

            through_items(e, item)

        @block.vector
        def _(e):
            def copy(S, job, out, in_):
                S.wait_full(e, job)
                S.freed(e.tensor_copy(out, in_), job)

            def split_low(L, w):
                c, gw = C_OF[w], L * NW_LAYER + w
                e.wait_ge(hi_ready, gw + 1)
                s = w_split[gw % SRING]
                e.tensor_tensor(s[:, 1, :], view(slot(c), CH), s[:, 0, :].bitcast(F32), ALU.subtract).then_inc(lo_ready, 1)

            def split_norm(L, i):
                for k in range(KT):
                    e.wait_ge(xh_ready.sem, xh_ready.at(L, 8 * i + k + 1))
                    e.tensor_tensor(xn_split[:, 1, k, :], xn[:, k, :], xn_split[:, 0, k, :].bitcast(F32), ALU.subtract)\
                        .then_inc(xl_ready.sem, 1)

            def norm(L, S, i, w=None):
                if w is not None:
                    split_low(L, w)
                S.wait_read(e, ("ssq", i))
                e.reciprocal(rstd, rms).then_inc(rstd_ready.sem, 1)
                e.wait_ge(rstd_ready.sem, rstd_ready.at(L, i + 1))
                for k in range(KT):
                    e.scalar_tensor_tensor(out=xn[:, k, :], in0=xT[:, k, :], scalar=gain[:, 8 * i + k:8 * i + k + 1], in1=rstd,
                                           op0=ALU.mult, op1=ALU.mult).then_inc(xn_ready.sem, 1)

            def add_to_x(S, name, tiles):
                for c in tiles:
                    job = (name, c)
                    S.wait_full(e, job)
                    S.freed(e.tensor_tensor(xT[:, c, :], xT[:, c, :], S.ps(job)[:, 0:T], ALU.add), job)

            def wait_x(S, name):
                for c in range(KT):
                    S.wait_read(e, (name, c))

            for b in range(8):
                e.sem_inc(free[b], 1)
            pre.wait_full(e, ("gain", 0))
            pre.freed(e.tensor_copy(gains, pre.ps(("gain", 0))[:, 0:LAYERS * N_GAIN].rearrange("p (l n) -> p l n", l=LAYERS)),
                      ("gain", 0))
            for tt, (a, n) in enumerate(TT):
                for hf in range(2):
                    job = ("x", tt, hf)
                    copy(pre, job, xT[:, 4 * hf:4 * hf + 4, a:a + n],
                         pre.ps(job).rearrange("p (k t) -> p k t", k=4)[:, :, 0:n])
            pre.wait_read(e, ("gain", 0))
            pre.wait_read(e, ("x", 2, 1))
            u_all = uflat[:, :, 16 + SEQ:].rearrange("p g (b s) -> p g b s", b=DB)

            def attention(L):
                S = att_sec(L)
                e.tensor_copy(gain, gains[:, L, :]).then_inc(gain_ready.sem, 1)
                e.wait_ge(gain_ready.sem, gain_ready.at(L, 1))
                e.tensor_scalar(q_gain, gain[:, N_GAIN - 2:N_GAIN - 1], HD ** -0.5, None, ALU.mult).then_inc(gain_ready.sem, 1)
                e.wait_ge(gain_ready.sem, gain_ready.at(L, 2))
                if L == 0:
                    split_low(0, 0)
                norm(L, S, 0, 1)
                split_norm(L, 0)
                e.wait_ge(ones_set, 3 + L)
                for c in range(PG):
                    if c == 2:
                        split_low(L, 2)
                    job = ("u", c)
                    S.wait_full(e, job)
                    ps = S.ps(job)
                    e.tensor_copy(uflat[:, c, 16:16 + SEQ], ps[:, 0:SEQ])
                    e.tensor_copy(u_new[:, c, :], ps[:, SEQ:T])
                    S.freed(e.tensor_copy(u_all[:, c, :, STATE:], ps[:, SEQ:T].rearrange("p (b t) -> p b t", b=DB)), job)

                def mean(g):
                    steps = sum(range(1, g + 2))
                    e.wait_ge(win_ready.sem, win_ready.at(L, steps))
                    w = window[(steps - 1) % 2]
                    e.tensor_tensor(first_mean, w[:, 16:32], inv_count[:, g, :], ALU.mult).then_inc(mean_ready.sem, 1)
                    e.scalar_tensor_tensor(out=pooled[:, g, 16:SEQ], in0=w[:, 32:16 + SEQ], scalar=1.0 / WINDOWS[g],
                                           in1=uflat[:, g, 32:16 + SEQ], op0=ALU.mult, op1=ALU.subtract)
                    e.scalar_tensor_tensor(
                        out=pooled[:, g, SEQ:T].rearrange("p (b t) -> p b t", b=DB),
                        in0=w[:, 16 + SEQ:UW].rearrange("p (b s) -> p b s", b=DB)[:, :, STATE:], scalar=1.0 / WINDOWS[g],
                        in1=u_all[:, g, :, STATE:], op0=ALU.mult, op1=ALU.subtract)
                    e.wait_ge(mean_ready.sem, mean_ready.at(L, 2 * g + 1))
                    e.tensor_tensor(pooled[:, g, 0:16], first_mean, uflat[:, g, 16:32], ALU.subtract)\
                        .then_inc(mean_ready.sem, 1)

                for c in range(24):
                    if c % 2 == 0:
                        split_low(L, c // 2 + 3)
                    if c == 20:
                        e.wait_ge(u_stored, 16 * U_STORES * (L + 1))
                    S.wait_read(e, ("qn", c))
                    r = head_rms[:, c % 4, :]
                    e.reciprocal(r, r).then_inc(hrstd_ready.sem, 1)
                    e.wait_ge(hrstd_ready.sem, hrstd_ready.at(L, c + 1))
                    S.wait_full(e, ("z", c))
                    out, g = (qT[:, c, :], q_gain) if c < 12 else (kT[:, c - 12, :], gain[:, N_GAIN - 1:N_GAIN])
                    S.freed(e.scalar_tensor_tensor(out=out, in0=S.ps(("z", c))[:, 0:T], scalar=g, in1=r,
                                                   op0=ALU.mult, op1=ALU.mult), ("z", c))
                    if c == 3:
                        copy(S, ("ut", 0), utok[0][0:STATE, :], S.ps(("ut", 0))[0:STATE])
                    if c == 5:
                        copy(S, ("ut", 1), utok[1][0:NS, :], S.ps(("ut", 1))[0:NS])
                    if c == 7:
                        S.wait_full(e, ("st", 0))
                        for g in range(PG):
                            r = e.tensor_copy(u_all[:, g, :, 0:STATE], S.ps(("st", 0))[:, 120 * g:120 * (g + 1)]
                                              .rearrange("p (b s) -> p b s", b=DB))
                        S.freed(r, ("st", 0))
                    if c in (13, 15, 17, 19):
                        mean((c - 13) // 2)

                i = 0
                for g in range(G):
                    split_low(L, 15 + 2 * g)
                    if g < 2:
                        split_low(L, 16 + 2 * g)
                    if g == 0:
                        for c in range(PG):
                            job = ("yp", c)
                            S.wait_full(e, job)
                            S.freed(e.tensor_scalar(poolT[:, c, :], S.ps(job)[:, 0:T], gain[:, 16 + c:17 + c], None, ALU.mult), job)
                    for gg, tt in K_STORES:
                        if gg == g:
                            n = TT[tt][1]
                            if i >= 2:
                                e.wait_ge(k_stored[i % 2], 16 * (L * (len(K_STORES) // 2) + i // 2))
                            copy(S, ("kt", g, tt), k_tok[0:n, i % 2, :], S.ps(("kt", g, tt))[0:n])
                            i += 1
                    for v in ((g - 1,) if g == 1 else (1, 2) if g == 2 else ()):
                        for tt, (_, n) in enumerate(TT):
                            copy(S, ("vt", v, tt), v_tok[0:n, tt, v, :], S.ps(("vt", v, tt))[0:n])

                for u in range(len(UNITS) + 3):
                    if u < len(UNITS):
                        j, qt, he = UNITS[u]
                        w = 128 * (qt + 1)
                        p = probs[u % 3]
                        for g in range(G):
                            n = 1 if qt and g == 2 else 0
                            at = 0 if n else g * w
                            if g == 0 or n:
                                S.wait_full(e, ("S", u, n))
                            r = e.scalar_tensor_tensor(out=p[:, g * w:(g + 1) * w], in0=dist[:, g, 256 - w:256],
                                                       scalar=-float(SLOPES[g, 2 * j + he]), in1=S.ps(("S", u, n))[:, at:at + w],
                                                       op0=ALU.mult, op1=ALU.add)
                            if g == 2 or (qt and g == 1):
                                S.freed(r, ("S", u, n))
                        for n in range(1 + qt):
                            S.wait_read(e, ("S", u, n))
                        e.tensor_reduce(stats[:, u:u + 1], p[:, 0:G * w], AX.X, ALU.max, negate=True).then_inc(max_ready.sem, 1)
                    if 1 <= u <= len(UNITS):
                        e.wait_ge(exp_ready.sem, exp_ready.at(L, u))
                        e.reciprocal(stats[:, 32 + u - 1:32 + u], stats[:, 16 + u - 1:16 + u]).then_inc(rden_ready.sem, 1)
                    if u >= 3 and UNITS[u - 3][2] == 1:
                        j, qt, _ = UNITS[u - 3]
                        copy(S, ("O", j, qt), attT[:, j, 128 * qt:128 * (qt + 1)], S.ps(("O", j, qt))[:, 0:128])

                def softmax_bias(half):
                    job = ("ss", half)
                    S.wait_full(e, job)
                    s = S.ps(job)[:, 0:G * 160].rearrange("p (g k) -> p g k", g=G)
                    p = s_probs[half]
                    e.tensor_tensor(p[:, :, 0:128], s[:, :, 0:128], bias_old, ALU.add)
                    S.freed(e.tensor_tensor(p[:, :, 128:160], s[:, :, 128:160], bias_new[:, half], ALU.add), job)
                    S.wait_read(e, job)
                    e.tensor_reduce(stats[:, half:half + 1], p.rearrange("p g k -> p (g k)"), AX.X, ALU.max, negate=True)\
                        .then_inc(s_max.sem, 1)

                def softmax_scale(half):
                    e.wait_ge(s_exp.sem, s_exp.at(L, half + 1))
                    e.reciprocal(stats[:, 32 + half:33 + half], stats[:, 16 + half:17 + half]).then_inc(s_rden.sem, 1)
                    e.wait_ge(s_rden.sem, s_rden.at(L, half + 1))
                    flat = s_probs[half].rearrange("p g k -> p (g k)")
                    e.tensor_scalar(flat, flat, stats[:, 32 + half:33 + half], None, ALU.mult).then_inc(s_p.sem, 1)

                def new_probs(half):
                    copy(S, ("pn", half), sp_new[half][0:NS], S.ps(("pn", half))[0:NS, 0:G * 128].rearrange("p (g r) -> p g r", g=G))

                def own_columns(half):
                    S.wait_full(e, ("OS", half))
                    S.freed(e.tensor_tensor(o_own, own_head, S.ps(("OS", half)), ALU.mult), ("OS", half))

                def sample_out(half):
                    at = SEQ + 16 * half
                    copy(S, ("ex", half), attT[:, :, at:at + 16], S.ps(("ex", half))[:, 0:64].rearrange("p (j s) -> p j s", j=J))

                e.wait_ge(v_stored, 16 * len(K_STORES) * (L + 1))
                for m in range(HB * NT):
                    if m % 2 == 1:
                        wait_cache_scored(e, L, S, m - 3)
                        copy(S, ("kT", m // NT, m % NT), cacheT[m % 3], S.ps(("kT", m // NT, m % NT))
                             .rearrange("p (j m) -> p j m", j=J))
                    if m == NT + MAX_AT:
                        softmax_bias(0)
                    if m == NT + SCALE_AT:
                        softmax_scale(0)
                    if m == NT + PT_AT + 1:
                        new_probs(0)
                softmax_bias(1)
                softmax_scale(1)
                new_probs(1)
                own_columns(0)
                sample_out(0)
                split_low(L, W_MERGE)
                split_low(L, W_MERGE + 1)
                own_columns(1)
                sample_out(1)

                for i in range(KT // 2):
                    if i >= 1:
                        split_low(L, W_MERGE + 3 * i + 1)
                    split_low(L, W_MERGE + 3 * i + 2)
                    if i == 0:
                        for b, src in enumerate((poolT, attT)):
                            e.wait_ge(bh_ready.sem, bh_ready.at(L, b + 1))
                            e.tensor_tensor(branch_split[:, b, 1], src, branch_split[:, b, 0].bitcast(F32), ALU.subtract)\
                                .then_inc(bl_ready.sem, 1)
                    split_low(L, W_MERGE + 3 * i + 3)
                    for x in range(2):
                        c = 2 * i + x
                        for b in range(2):
                            n = (2 * c + b) % 4
                            job = (("pb", "ab")[b], c)
                            if c >= 2:
                                e.wait_ge(merged_ready.sem, merged_ready.at(L, c - 1))
                            S.wait_read(e, (f"g{b}", c))
                            S.wait_full(e, job)
                            S.freed(e.tensor_tensor(prod[n], gate[n], S.ps(job)[:, 0:T], ALU.mult), job)
                for i in range(KT // 2):
                    if W_OUT + i + 1 < NW_ATT + (L == 0):
                        split_low(L, W_OUT + i + 1)
                    add_to_x(S, "wo", (2 * i, 2 * i + 1))
                wait_x(S, "wo")
                for i in range(2):
                    e.wait_ge(k_stored[i], 16 * (len(K_STORES) // 2) * (L + 1))

            def ffn():
                S = dense_sec
                norm(0, S, 1, W_UP + 1)
                split_norm(0, 1)
                for i in range(FT // 2):
                    if i >= 1:
                        split_low(0, W_UP + 2 * i + 1)
                    split_low(0, W_UP + 2 * i + 2)
                    for f in (2 * i, 2 * i + 1):
                        if f >= 4:
                            e.wait_ge(hl_ready, f - 3)
                        S.wait_read(e, ("fa", f))
                        S.wait_full(e, ("fb", f))
                        S.freed(e.tensor_tensor(hid[f % 4], up_a[f % 4], S.ps(("fb", f))[:, 0:T], ALU.mult), ("fb", f))
                for w in range(W_DOWN + 1, NW_LAYER):
                    split_low(0, w)
                split_low(1, 0)
                add_to_x(S, "fd", range(KT))
                wait_x(S, "fd")

            attention(0)
            ffn()
            attention(1)

            P = prep
            norm(1, P, 1)
            steps = {"n": 0}

            def step(instruction, wait=True):
                instruction.then_inc(route, 1)
                steps["n"] += 1
                if wait:
                    e.wait_ge(route, steps["n"])

            for tt, (_, n) in enumerate(TT):
                for hf in range(2):
                    job = ("xt", tt, hf)
                    copy(P, job, x_tok[0:n, tt, 512 * hf:512 * (hf + 1)], P.ps(job)[0:n])
            step(e.memset(logits, 0.0))
            for tt, (_, n) in enumerate(TT):
                copy(P, ("rl", tt), logits[0:n, tt, :], P.ps(("rl", tt))[0:n, 0:NE])
            for tt in range(3):
                P.wait_read(e, ("rl", tt))
            for tt in range(3):
                step(e.max(best[:, tt, :], logits[:, tt, :]), tt == 2)
            for tt in range(3):
                step(e.max_index(best_at[:, tt, :], best[:, tt, :], logits[:, tt, :]), tt == 2)
            step(e.tensor_copy(best_f, best_at))
            step(e.tensor_tensor(gap, best[:, :, 1:2], best[:, :, 0:1], ALU.subtract))
            assert steps["n"] == R_GAP
            e.wait_ge(gap_done, 1)
            step(e.tensor_scalar(gap_sum, gap_exp, 1.0, None, ALU.add))
            step(e.reciprocal(gate1, gap_sum))
            step(e.tensor_tensor(gate2, gap_exp, gate1, ALU.mult))
            e.wait_ge(moe_small, 16)
            for n, hit in enumerate((hit1, hit2)):
                for tt in range(3):
                    step(e.tensor_scalar(hit[:, tt, :], iota[:, 0:NE], best_f[:, tt, n:n + 1], real[:, tt:tt + 1],
                                         ALU.is_equal, ALU.mult), tt == 2)
            step(e.tensor_tensor(chosen, hit1, hit2, ALU.add))
            assert steps["n"] == R_CHOSEN
            for hit, gv, out in ((hit1, gate1, gate_a), (hit2, gate2, gate_b)):
                for tt in range(3):
                    step(e.tensor_scalar(out[:, tt, :], hit[:, tt, :], gv[:, tt, :], None, ALU.mult), tt == 2)
            by_block = gate_of.rearrange("p t (e b) -> p t e b", b=BLOCKS)
            for b in range(BLOCKS):
                step(e.tensor_tensor(by_block[:, :, :, b], gate_a, gate_b, ALU.add), b == BLOCKS - 1)
            for tt in range(3):
                job = ("pos", tt)
                P.wait_full(e, job)
                P.freed(e.scalar_tensor_tensor(out=place_1[:, tt, :], in0=P.ps(job)[:, 0:NE], scalar=1.0,
                                               in1=chosen[:, tt, :], op0=ALU.add, op1=ALU.mult), job)
            copy(P, ("cnt", 0), counts, P.ps(("cnt", 0))[:, 0:NE])
            for tt in range(3):
                P.wait_read(e, ("pos", tt))
            P.wait_read(e, ("cnt", 0))
            by_block = slot_of.rearrange("p t (e b) -> p t e b", b=BLOCKS)
            flag_by = flag_f.rearrange("p (e b) -> p e b", b=BLOCKS)
            for b in range(BLOCKS):
                step(e.tensor_scalar(by_block[:, :, :, b], place_1, -(1.0 + 128 * b), None, ALU.add), False)
                step(e.tensor_scalar(flag_by[:, :, b], counts, 128.0 * b, None, ALU.is_gt if b else ALU.is_ge), b == BLOCKS - 1)
            step(e.tensor_tensor_scan(flag_sum[0:1, :], ones[0:1, 0:ITEMS], flag_f[0:1, :], 0.0, ALU.mult, ALU.add))
            step(e.tensor_copy(flags_i[0:1, 0, :], flag_f[0:1, :]), False)
            e.tensor_tensor(flags_i[0:1, 1, :], flag_sum[0:1, :], flag_f[0:1, :], ALU.subtract).then_inc(flags_ready, 1)
            e.wait_ge(flags_ready, 1)

            def item(i, seq):
                I = item_sec(seq)
                for out, scale in ((onehot, False), (gated, True)):
                    for tt in range(3):
                        s1 = slot_of[:, tt, bass.ds(i, 1)]
                        if scale:
                            r = e.tensor_scalar(out[:, tt, :], iota, s1, gate_of[:, tt, bass.ds(i, 1)], ALU.is_equal, ALU.mult)
                        else:
                            r = e.tensor_scalar(out[:, tt, :], iota, s1, None, ALU.is_equal)
                        r.then_inc(m_hot, 1)

                def expert_low(v):
                    if v >= N_EXPERT:
                        return
                    e.wait_ge(hi_ready, NW + seq * N_EXPERT + v + 1)
                    w = e_split[v % MSRING]
                    e.tensor_tensor(w[:, 1, :], view(slot(v, MRING), CH), w[:, 0, :].bitcast(F32), ALU.subtract)\
                        .then_inc(lo_ready, 1)

                def low(job, n, hi, out):
                    e.wait_ge(eh_ready, 9 * seq + n)
                    I.freed(e.tensor_tensor(out, I.ps(job).rearrange("p (k s) -> p k s", k=4), hi.bitcast(F32), ALU.subtract), job)

                expert_low(0)
                expert_low(1)
                for n in range(2):
                    low(("xe", n), n + 1, xe_split[:, 0, 4 * n:4 * n + 4, :], xe_split[:, 1, 4 * n:4 * n + 4, :])
                for c in range(7):
                    for v in range(4 * c + 2, 4 * c + 5):
                        expert_low(v)
                    I.wait_read(e, ("eg", c))
                    I.wait_full(e, ("eu", c))
                    I.freed(e.tensor_tensor(m_h[c % 2], m_sig[c % 2], I.ps(("eu", c)), ALU.mult), ("eu", c))
                    expert_low(4 * c + 5)
                    if c >= 1:
                        low(("ht", c - 1), c + 2, hT_split[:, 0, 4 * c - 4:4 * c, :], hT_split[:, 1, 4 * c - 4:4 * c, :])
                for v in range(28, N_EXPERT):
                    expert_low(v + 2)
                    if v == 29:
                        low(("ht", 6), 9, hT_split[:, 0, 24:28, :], hT_split[:, 1, 24:28, :])
                copy(I, ("ed", 1), ye[:, 512:D], I.ps(("ed", 1)))
                I.wait_full(e, ("gst", 0))
                g = I.ps(("gst", 0)).rearrange("p (t n) -> p t n", t=4)
                e.tensor_copy(gatedT[:, 0:2, :], g[:, 0:2, :])
                I.freed(e.tensor_copy(gatedT[:, 2, 0:NS], g[:, 2, 0:NS]), ("gst", 0))
                for tt, (_, n) in enumerate(TT):
                    for hf in range(2):
                        job = ("co", tt, hf)
                        x = x_tok[0:n, tt, 512 * hf:512 * (hf + 1)]
                        item_before(seq).wait_read(e, job)
                        I.wait_full(e, job)
                        I.freed(e.tensor_tensor(x, x, I.ps(job)[0:n], ALU.add), job)

            through_items(e, item)
            e.memset(stats[:, 0:1], 0.0).then_inc(combined, 1)

        @block.gpsimd
        def _(e):
            e.memset(ones, 1.0).then_inc(ones_set, 1)
            e.memset(eps, EPS).then_inc(ones_set, 1)
            e.memset(uflat, 0.0).then_inc(ones_set, 1)
            e.wait_ge(ones_set, 3)
            pre.wait_read(e, ("x", 2, 1))

            def attention(L):
                S = att_sec(L)
                e.dma_start(stateraw[0:DB * STATE, :], io["state_pool"][L].rearrange("b s c -> (b s) c")).then_inc(state_loaded, 16)
                e.dma_start(w_pool, io["w_pool"][L].rearrange("g c d -> c g d")).then_inc(wpool_loaded, 16)
                e.dma_start(io["pool_sample"][L, :, 0:STATE - DS, :], io["state_pool"][L, :, DS:STATE, :]).then_inc(copied, 16)

                S.wait_read(e, ("ut", 0))
                e.dma_start(io["pool_prompt"][L, 0], utok[0][0:STATE, :]).then_inc(u_stored, 16)
                S.wait_read(e, ("ut", 1))
                for b in range(DB):
                    e.dma_start(io["pool_sample"][L, b, STATE - DS:STATE, :], utok[1][DS * b:DS * (b + 1), :])\
                        .then_inc(u_stored, 16)

                S.wait_read(e, ("st", 0))
                n = 0
                for g in range(PG):
                    src = uflat[:, g, :]
                    if g >= 1:
                        e.wait_ge(mean_ready.sem, mean_ready.at(L, 2 * g))
                    for s in range(g + 1):
                        lo, back = 2 ** (s + 1) - 1, 2 ** s
                        dst = window[n % 2]
                        e.tensor_tensor(dst[:, lo:UW], src[:, lo:UW], src[:, lo - back:UW - back], ALU.add)\
                            .then_inc(win_ready.sem, 1)
                        n += 1
                        e.wait_ge(win_ready.sem, win_ready.at(L, n))
                        src = dst

                i = 0
                for g in range(G):
                    for gg, tt in K_STORES:
                        if gg == g:
                            S.wait_read(e, ("kt", g, tt))
                            store_rows(L, g, tt, 0, k_tok[:, i % 2, :], k_stored[i % 2])
                            i += 1
                    for v in ((g - 1,) if g == 1 else (1, 2) if g == 2 else ()):
                        for gg, tt in K_STORES:
                            if gg == v:
                                S.wait_read(e, ("vt", v, tt))
                                store_rows(L, v, tt, 1, v_tok[:, tt, v, :], v_stored)

                S.wait_read(e, ("vt", 2, 2))
                e.memset(view(strips_at, 12 * ROWS + 2 * J * BH * DS * 32), 0.0).then_inc(zeroed.sem, 1)

                def scale(u):
                    w = 128 * G * (UNITS[u][1] + 1)
                    e.wait_ge(rden_ready.sem, rden_ready.at(L, u + 1))
                    e.tensor_scalar(probs[u % 3][:, 0:w], probs[u % 3][:, 0:w], stats[:, 32 + u:33 + u], 1.0,
                                    ALU.mult, ALU.mult).then_inc(p_ready.sem, 1)

                def place_queries(half):
                    at = SEQ + 16 * half
                    for he in range(2):
                        p = slice(64 * he, 64 * he + 64)
                        for j in range(J):
                            h = 2 * j + he
                            src = qT.rearrange("p (g j) t -> p g j t", g=G)[p, :, j, at:at + 16]
                            e.tensor_copy(q_all.rearrange("p (g j) b t h -> p g j (b t) h", g=G)[p, :, j, :, h], src)\
                                .then_inc(filled.sem, 1)
                            one = view(q_one_at, 2 * J * BH * DS * 32)[p, :]
                            e.tensor_copy(strided(one, j * BH * DS * 32 + h, (J * BH * DS * 32, 2), (128, BH), (32 + H, DS)),
                                          src[:, 1:G].rearrange("p g (b t) -> p g b t", b=BH)).then_inc(filled.sem, 1)

                for u in range(len(UNITS)):
                    scale(u)
                e.wait_ge(zeroed.sem, zeroed.at(L, 1))
                e.wait_ge(p_ready.sem, p_ready.at(L, 16))
                place_queries(0)
                S.wait_read(e, ("O", J - 1, 1))
                e.wait_ge(v_stored, 16 * len(K_STORES) * (L + 1))
                e.wait_ge(filled.sem, filled.at(L, 16))
                for a in sp_at:
                    e.memset(view(a + ROWS, 1024), 0.0).then_inc(zeroed.sem, 1)
                e.memset(stats[:, 46:47], 0.0).then_inc(zeroed.sem, 1)
                e.wait_ge(zeroed.sem, zeroed.at(L, 4))
                S.wait_full(e, ("ss", 0))
                place_queries(1)
                e.wait_ge(filled.sem, filled.at(L, 32))
                for c in range(KT):
                    if c == 0:
                        S.wait_full(e, ("ss", 1))
                    for b in range(2):
                        S.wait_read(e, (("pb", "ab")[b], c))
                    e.tensor_tensor(merged[:, c, :], prod[(2 * c) % 4], prod[(2 * c + 1) % 4], ALU.add)\
                        .then_inc(merged_ready.sem, 1)
                    if c >= 2:
                        merge_low(L, c - 2)
                merge_low(L, KT - 2)
                merge_low(L, KT - 1)
                S.wait_read(e, ("wo", KT - 1))

            def merge_low(L, c):
                e.wait_ge(mh_ready.sem, mh_ready.at(L, c + 1))
                e.tensor_tensor(merged_split[:, 1, c, :], merged[:, c, :], merged_split[:, 0, c, :].bitcast(F32), ALU.subtract)\
                    .then_inc(ml_ready.sem, 1)

            def store_rows(L, g, tt, kv, rows, signal):
                a, n = TT[tt]
                if tt == 2:
                    dst = io[f"kv{g}_sample"][L].rearrange("b t v h d -> (b t) v (h d)")[:, kv]
                else:
                    keep = min(SPAN[g], SEQ)
                    a -= SEQ - keep
                    dst = io[f"kv{g}_prompt"][L, 0, a:a + n, kv].rearrange("t h d -> t (h d)")
                e.dma_start(dst, rows[0:n, :]).then_inc(signal, 16)

            def ffn():
                for f in range(FT):
                    e.wait_ge(hh_ready, f + 1)
                    e.tensor_tensor(hid_split[:, 1, f, :], hid[f % 4], hid_split[:, 0, f, :].bitcast(F32), ALU.subtract)\
                        .then_inc(hl_ready, 1)
                for c in range(KT):
                    dense_sec.wait_read(e, ("fd", c))
                e.memset(uflat, 0.0).then_inc(ones_set, 1)

            attention(0)
            ffn()
            attention(1)


_INS = ["x_prompt", "x_sample", "state_pool", "cache_kv_g0", "cache_kv_g1", "cache_kv_g2", "norm_attn", "w_in", "q_norm",
        "k_norm", "w_pool", "pool_scale", "w_branch_pool", "w_branch_attn", "w_out", "norm_ffn", "w1_dense", "w3_dense",
        "w2_dense", "router_w", "router_b", "we_gate", "we_up", "we_down"]
_OUTS = [("y_prompt", (1, SEQ, D)), ("y_sample", (DB, DS, D)), ("pool_prompt", (LAYERS, 1, STATE, POOL_W)),
         ("pool_sample", (LAYERS, DB, STATE, POOL_W))]
for _g in range(G):
    _OUTS += [(f"kv{_g}_prompt", (LAYERS, 1, min(SPAN[_g], SEQ), 2, H, HD)), (f"kv{_g}_sample", (LAYERS, DB, DS, 2, H, HD))]


def kernel(**inputs):
    import concourse.bacc as bacc
    from concourse.bass_utils import run_bass_kernel_spmd

    nc = bacc.Bacc("TRN2", target_bir_lowering=False, num_devices=1)
    const_a, const_m = shape_constants()
    arrays = {"in_" + n: np.ascontiguousarray(inputs[n]) for n in _INS}
    arrays["in_const_a"], arrays["in_const_m"] = const_a, const_m
    io = {n[3:]: nc.dram_tensor(n, a.shape, mybir.dt.from_np(a.dtype), kind="ExternalInput").ap() for n, a in arrays.items()}
    for name, shape in _OUTS:
        io[name] = nc.dram_tensor("out_" + name, shape, F32, kind="ExternalOutput").ap()
    build(nc, io)
    r = run_bass_kernel_spmd(nc, [arrays], core_ids=[0])
    return tuple(r.results[0]["out_" + name] for name, _ in _OUTS)
```

```python
import numpy as np
from contextlib import ExitStack
import concourse.bass as bass
from concourse import mybir
from concourse.alu_op_type import AluOpType as ALU

F32 = mybir.dt.float32
I32 = mybir.dt.int32
U32 = mybir.dt.uint32
F32R = mybir.dt.float32r
ACT = mybir.ActivationFunctionType
AX = mybir.AxisListType

PART = 128
D = 1024
KT = D // PART
SEQ, DB, DS = 256, 8, 4
NS = DB * DS
T = SEQ + NS
LAYERS = 2
H, HD, G = 8, 64, 3
GW = H * HD
J = GW // PART
QKV = G * GW
HEADS = G * H
POOL_W = 512
PG = POOL_W // PART
IN_COLS = POOL_W + 3 * QKV + 2 * D
WINDOWS = (2, 4, 8, 16)
DIL = (1, 4, 16)
SPAN = (128, 512, 2048)
STATE = 15
FF = 2816
FT = FF // PART
NE, FE = 8, 3584
ET = FE // PART
EPS = 1e-6
MASKED = 1e33
NEG = -1e30

CH = 2048
RING = 5
MRING = 7
SRING = 2
MSRING = 3
HB = 2
BH = DB // HB
ROWS = BH * DS * H
TT = ((0, 128), (128, 128), (256, 32))
BLOCKS = 3
EXTRA = NE * (BLOCKS - 1)
ITEMS = NE + EXTRA
LOW, HIGH = 41216, 11984

SLOPES = np.exp2(-8.0 * np.arange(1, G * H + 1) / (G * H)).astype(np.float32).reshape(G, H)


def shape_constants():
    p, f = np.arange(PART)[:, None], np.arange(PART)[None, :]
    ident = (p == f)
    band = (np.arange(2 * HEADS)[None, :] == HEADS + p // HD)
    dist = np.full((PART, G, 2, PART), MASKED)
    for g in range(G):
        for kind in range(2):
            d = p - f + PART * (1 - kind)
            ok = (d >= 0) & (d <= SPAN[g]) & (d % DIL[g] == 0)
            dist[:, g, kind] = np.where(ok, d, MASKED)
    inv = np.zeros((PART, PG, 16))
    for g, w in enumerate(WINDOWS):
        inv[:, g] = 1.0 / np.minimum(np.arange(16) + 1, w)
    row = np.arange(ROWS)
    b, t, h = row // (DS * H), row // H % DS, row % H
    old = np.full((ROWS, G, PART), NEG)
    new = np.full((ROWS, HB, G, NS), NEG)
    key = np.arange(PART)
    kb, kt = np.arange(NS) // DS, np.arange(NS) % DS
    for g in range(G):
        dd = (PART + t[:, None] * (g == 0) - key[None, :]) * DIL[g]
        ok = (key[None, :] >= t[:, None]) | (g > 0)
        old[:, g] = np.where(ok, -SLOPES[g][h][:, None] * dd, NEG)
        for half in range(HB):
            dn = t[:, None] - kt[None, :]
            ok = (kb[None, :] == b[:, None] + half * BH) & ((dn >= 0) if g == 0 else (dn == 0))
            new[:, half, g] = np.where(ok, -SLOPES[g][h][:, None] * dn, NEG)
    own = (np.arange(GW)[None, :] // HD == h[:, None])
    pick = (row[:, None] // H == np.arange(BH * DS)[None, :])
    a = np.concatenate([x.reshape(PART, -1) for x in (ident, band, dist, inv, old, new, own, pick)], axis=1)
    real = np.stack([np.arange(PART) < n for _, n in TT], axis=1)
    m = np.concatenate([(p < f).astype(float), np.broadcast_to(f, (PART, PART)), real], axis=1)
    spread = (np.arange(HEADS)[:, None] == np.arange(12 * PART)[None, :] // HD)
    return a.astype(np.float32), m.astype(np.float32), spread.astype(np.float32).reshape(HEADS, 3, GW)


def chunk_kinds():
    return ["W"] * N_IN + ["C"] * N_CACHE + ["W"] * (N_MERGE + N_DENSE)


class Tally:

    def __init__(self, sem, layer, before=0):
        self.sem, self.layer, self.before = sem, layer, before

    def at(self, L, n):
        return self.before + L * self.layer + n


class Banks:

    def __init__(self):
        self.where, self.uses, self.turn = {}, [0] * 8, {}

    def put(self, name, pool=tuple(range(8))):
        n = self.turn.get(pool, 0)
        self.turn[pool] = n + 1
        bank = pool[n % len(pool)]
        self.where[name] = (bank, self.uses[bank])
        self.uses[bank] += 1


KPOOL, ST_BANKS, O_BANKS, UPOOL, UKPOOL = (0, 1, 2, 3), (5, 4), (6, 7), (0, 1, 2, 3, 4), (6, 7)


def prompt_units():
    return [(j, qt, e) for j in range(J) for qt in range(2) for e in range(2)]


UNITS = prompt_units()
K_STORES = [(g, tt) for g in range(G) for tt in range(3) if (g, tt) != (0, 0)]


def cache_tiles():
    out = [(0, b, 0, b, None) for b in range(BH)]
    for g in (1, 2):
        for b in range(BH):
            out += [(1 + BH * (g - 1) + b, t, g, b, t) for t in range(DS)]
    return out


TILES = cache_tiles()
NT = len(TILES)
FIRST_UNIT = 3


def unit_tiles(u):
    at = 2 * (u - FIRST_UNIT)
    return [m for m in (at, at + 1) if 0 <= m < NT]


REST = unit_tiles(len(UNITS) + 2)[-1] + 1
MAX_AT, EXP_AT, SCALE_AT, PT_AT = 3, 6, 9, 14
PT1_AT, EX_AT = 12, 6
AFTER = {5: [("ut", 0)], 7: [("ut", 1)], 9: [("st", 0)], 27: [("yp", c) for c in range(PG)]}
for _i in range(6):
    AFTER[16 + _i] = [("bc", 2 * _i), ("bc", 2 * _i + 1)]
    AFTER.setdefault(28 + _i, []).extend([("bc", 12 + 2 * _i), ("bc", 13 + 2 * _i)])
ROW_TILES = {31: [("kt", 0), ("vt", 0)], 32: [("vt", 1)], 34: [("kt", 1)], 35: [("kt", 2), ("vt", 2)]}
for _n, _kinds in ROW_TILES.items():
    for _kind, _g in _kinds:
        AFTER.setdefault(_n, []).extend((_kind, _g, tt) for tt in range(3) if (_kind, _g, tt) != ("kt", 0, 0))
MEAN_AT = (14, 18, 22, 26)
SIX, SUMS = (0, 1, 2, 3, 4, 5), (6, 7)


def section_pre():
    return [(("gain", 0), None)] + [(("x", tt, hf), None) for tt in range(3) for hf in range(2)]


def column_job(n):
    return ("z", n) if n < 24 else ("zv", n - 24)


def section_attention():
    js = [(("ssq", 0), None)]
    js += [(("u", c), None) for c in range(PG)]
    for n in range(36):
        if n in (2, 14):
            js.append((("hs", n // 12), SUMS))
        js.append((column_job(n), SIX))
        js += [(job, SIX) for job in AFTER.get(n, [])]
    for u in range(len(UNITS) + 3):
        if u < len(UNITS):
            js += [(("S", u, n), UPOOL) for n in range(1 + UNITS[u][1])]
        if 2 <= u < len(UNITS) + 2:
            js += [(("T", u - 2, n), UPOOL) for n in range(1 + UNITS[u - 2][1])]
        if u >= 3 and UNITS[u - 3][2] == 0:
            js.append((("O", UNITS[u - 3][0], UNITS[u - 3][1]), UPOOL))
        js += [(("kT", 0, m), UKPOOL) for m in unit_tiles(u)]
    for half in range(HB):
        js.append((("ss", half), ST_BANKS))
        for n in range(0 if half else REST, NT):
            js.append((("kT", half, n), KPOOL))
            if half == 1 and n == PT_AT:
                js += [(("pt", 0), KPOOL), (("pn", 0), KPOOL)]
    for half in range(HB):
        js.append((("OS", half), O_BANKS))
        js += [(("pt", 1), KPOOL), (("pn", 1), KPOOL)] if half == 0 else [(("ex", 0), KPOOL)]
    for i in range(KT // 2):
        js += [((name, 2 * i + x), None) for name in ("g0", "g1") for x in range(2)]
        if i == 0:
            js.append((("ex", 1), KPOOL))
        js += [((name, 2 * i + x), None) for x in range(2) for name in ("pb", "ab")]
    js += [(("wo", c), None) for c in range(KT)]
    return js


def section_dense():
    js = [(("ssq", 1), None)]
    for i in range(FT // 2):
        js += [((name, 2 * i + x), None) for name in ("fa", "fb") for x in range(2)]
    return js + [(("fd", c), None) for c in range(KT)]


def section_moe_prep():
    js = [(("ssq", 1), None)]
    js += [(("xt", tt, hf), None) for tt in range(3) for hf in range(2)]
    js += [(("xnt", tt, hf), None) for tt in range(3) for hf in range(2)]
    js += [(("rl", tt), None) for tt in range(3)]
    return js + [(("pos", tt), None) for tt in range(3)] + [(("cnt", 0), None)]


ROTATE, PAIR = (0, 1, 2, 3, 4, 5), (6, 7)


def rows_of(name):
    return [((name, tt, hf), PAIR) for tt in range(3) for hf in range(2)]


def section_moe_gather():
    return [(("xe", n), PAIR) for n in range(2)]


def section_moe_item(before, ahead):
    js = [(("eg", 0), ROTATE), (("eu", 0), ROTATE)]
    if before:
        js += rows_of("cb")
    if ahead:
        js.append((("gst", 0), ROTATE))
    for c in range(1, 7):
        js += [(("eg", c), ROTATE), (("eu", c), ROTATE), (("ht", c - 1), ROTATE)]
    js += [(("ed", 0), ROTATE), (("ed", 1), ROTATE), (("ht", 6), ROTATE)]
    return js + (section_moe_gather() if ahead else [(("gst", 0), ROTATE)] + rows_of("co"))


def plan(sections):
    b, out = Banks(), {}
    for name, section in sections:
        b.turn, start = {}, list(b.uses)
        b.where = {}
        for job, pool in section:
            b.put(job, pool or tuple(range(8)))
        out[name] = (dict(b.where), start, [x - y for x, y in zip(b.uses, start)])
    return out


N_GAIN = 2 * KT + PG + 2

N_IN = (IN_COLS - 2 * D) // 256
N_CACHE = 2 * HB * (1 + 2 * BH)
N_MERGE = 3 * KT // 2 + KT // 2
N_ATT = N_IN + N_CACHE + N_MERGE
N_UP, N_DOWN = 2 * (FF // 256), FT // 2
N_DENSE = N_UP + N_DOWN
N_LAYER = N_ATT + N_DENSE
N_EXPERT = 3 * (FE // 256)
C_CACHE, C_MERGE, C_UP, C_DOWN = N_IN, N_IN + N_CACHE, N_ATT, N_ATT + N_UP
assert N_LAYER % RING == 0 and N_EXPERT % MRING == 0 and N_EXPERT % MSRING == 0
N_SMALL = 7
R_GAP, R_CHOSEN = 9, 19
U_STORES = 1 + DB
KINDS = chunk_kinds()
C_OF = [c for c, kind in enumerate(KINDS) if kind == "W"]
W_OF = {c: w for w, c in enumerate(C_OF)}
NW_LAYER, NW_ATT = len(C_OF), sum(kind == "W" for kind in KINDS[:N_ATT])
NW = NW_LAYER + NW_ATT
W_MERGE, W_OUT, W_UP, W_DOWN = N_IN, N_IN + 3 * KT // 2, NW_ATT, NW_ATT + N_UP
DMAS = [1] * (N_IN + N_CACHE) + [1, 1, 2] * (KT // 2) + [1] * (KT // 2 + N_DENSE)
assert len(DMAS) == N_LAYER


def dmas_until(n, s):
    return sum(DMAS[c] for c in range(n) if c % RING == s)



def build(nc, io):
    plans = plan([("pre", section_pre()), ("att", section_attention()), ("dense", section_dense())])
    pre_uses = plans["pre"][2]
    layer_uses = [a + b for a, b in zip(plans["att"][2], plans["dense"][2])]
    moe_start = [p + l + a for p, l, a in zip(pre_uses, layer_uses, plans["att"][2])]
    mplans = plan([("prep", section_moe_prep() + section_moe_gather()), ("first", section_moe_item(False, True)),
                   ("steady", section_moe_item(True, True)), ("last", section_moe_item(True, False)),
                   ("extra", section_moe_gather() + section_moe_item(False, False))])

    ctx = ExitStack()
    with ctx:
        sem = lambda name: ctx.enter_context(nc.semaphore(name))
        low_part = ctx.enter_context(nc.sbuf_tensor("low_part", [PART, LOW], F32))
        high_part = ctx.enter_context(nc.sbuf_tensor("high_part", [PART, HIGH], F32))
        psum = ctx.enter_context(nc.psum_tensor("psum", [PART, 8, 512], F32))
        place = {"at": 0}

        def take(n, at=None):
            if at is None:
                at = place["at"]
                place["at"] = at + -(-n // 8) * 8
            return at

        def view(at, *shape):
            n = int(np.prod(shape))
            assert at + n <= LOW or LOW <= at and at + n <= LOW + HIGH, (at, n)
            flat = low_part[:, at:at + n] if at < LOW else high_part[:, at - LOW:at - LOW + n]
            if len(shape) == 1:
                return flat
            names = "abcd"[:len(shape)]
            kw = {names[i]: shape[i] for i in range(1, len(shape))}
            return flat.rearrange(f"p ({' '.join(names)}) -> p {' '.join(names)}", **kw)

        split_base = nc.sbuf_base - 4 * (LOW + HIGH)

        def split_view(name, at, *shape):
            t = nc.alloc_sbuf_tensor_at(name, [PART, int(np.prod(shape))], F32R, offset=split_base + 4 * at)
            names = "abcd"[:len(shape)]
            kw = {names[i]: shape[i] for i in range(1, len(shape))}
            return t[:, :].rearrange(f"p ({' '.join(names)}) -> p {' '.join(names)}", **kw)

        def strided(base, skip, *dims):
            return bass.AP(base.tensor, base.offset + skip, [list(base.ap[0])] + [list(d) for d in dims])

        ring_at = take(RING * CH)
        ws_at = take(SRING * 2 * CH)
        xs_at = take(2 * KT * T)
        q_at = take(12 * T)
        k_at = take(12 * T)
        v_at = take(9 * 512)
        att_at = take(J * T)
        pool_at = take(PG * T)
        p_at = take(5 * 768)
        w_pool_at = take(PG * 128)
        w_pool = view(w_pool_at, PG, 128)
        assert place["at"] <= LOW, place["at"]
        const_at = place["at"] = low_end = LOW
        ident = view(take(128), 128)
        band = view(take(2 * HEADS), 2 * HEADS)
        dist = view(take(G * 2 * 128), G, 2 * 128)
        inv_count = view(take(PG * 16), PG, 16)
        bias_old = view(take(G * 128), G, 128)
        bias_new = view(take(HB * G * NS), HB, G, NS)
        own_head = view(take(GW), GW)
        pick = view(take(BH * DS), BH * DS)
        const_end = place["at"]
        ones = view(take(128), 128)
        eps = view(take(1), 1)
        gains = view(take(LAYERS * N_GAIN), LAYERS * N_GAIN)
        gain = view(take(N_GAIN), N_GAIN)
        q_gain = view(take(1), 1)
        router = view(take(KT * NE), KT, NE)
        router_bias = view(take(NE), NE)
        stats = view(take(48), 48)
        k_tok_at = take(2 * 512)
        k_tok = view(k_tok_at, 2, 512)
        xT_at = take(KT * T)
        xT = view(xT_at, KT, T)
        UW = 16 + SEQ + DB * (STATE + DS)
        strips_at = take(PG * UW)
        uflat = view(strips_at, PG, UW)
        work_at = take(KT * T)
        work = view(work_at, KT, T)
        head_rms = view(take(2 * T), 2, T)
        rms = view(take(T), T)
        rstd = view(take(T), T)
        place["at"] = max(place["at"], strips_at + 12 * ROWS + 2 * J * BH * DS * 32)
        assert place["at"] <= LOW + HIGH, place["at"]
        w_split = [split_view(f"w_split{i}", ws_at + 2 * CH * i, 2, CH) for i in range(SRING)]
        xn = work
        xn_split = split_view("xn_split", xs_at, 2, KT, T)
        qT, kT = view(q_at, 12, T), view(k_at, 12, T)
        v_tok = view(v_at, 3, G, 512)
        attT = view(att_at, J, T)
        poolT = view(pool_at, PG, T)
        probs = [view(p_at + 768 * i, 768) for i in range(3)]
        probsT = [view(p_at + 768 * (3 + i), 768) for i in range(2)]
        head_sq = view(work_at, 4, T)
        vT = [view(work_at + (4 - 4 * (g % 2)) * T, 4, T) for g in range(G)]
        window = [view(p_at + 768 * i, UW) for i in range(2)]
        first_mean = view(p_at + 768 * 2, 16)
        pooled = view(p_at + 768 * 3, PG, T)
        stateraw = view(pool_at, 512)
        utok = [view(p_at + 1600, 512), view(k_at + 8 * T, 512)]
        gain_raw = view(p_at, 128)
        u_new = view(p_at + 2112, PG, NS)
        q_all = view(strips_at, 12, BH, DS, H)
        q_one_at = strips_at + 12 * ROWS
        q_one = view(q_one_at, 2 * J, BH * DS, 32)
        assert 12 * ROWS + 2 * J * BH * DS * 32 <= place["at"] - strips_at
        s_probs = [view(p_at + 480 * i, G, 160) for i in range(HB)]
        sp_at = [p_at + 960, v_at]
        sp_all = [view(a, BH, DS * H) for a in sp_at]
        sp_one = [view(a + ROWS, 2, BH * DS, 32) for a in sp_at]
        sp_new = [view(a + ROWS + 1024, G, ROWS) for a in sp_at]
        o_own = view(p_at + 2496, GW)
        cacheT = [view(a, J, 128) for a in (w_pool_at, k_tok_at, k_tok_at + 512)]
        gate = [view(q_at + T * i, T) for i in range(4)]
        prod = [view(q_at + T * (4 + i), T) for i in range(4)]
        merged_split = split_view("merged_split", q_at + 8 * T, 2, KT, T)
        branch_split = split_view("branch_split", v_at, 2, 2, 4, T)
        merged = view(strips_at, KT, T)
        hid_split = split_view("hid_split", q_at, 2, FT, T)
        up_a = [view(p_at + T * i, T) for i in range(4)]
        hid = [view(p_at + T * (4 + i), T) for i in range(4)]
        x_raw = view(q_at, 3, D)
        slots = [ring_at + CH * i for i in range(MRING)]

        m = {"at": ring_at + MRING * CH}

        def mtake(n):
            at = m["at"]
            m["at"] = at + -(-n // 8) * 8
            assert m["at"] <= low_end, m["at"]
            return at

        e_split = [split_view(f"expert_split{i}", mtake(2 * CH), 2, CH) for i in range(MSRING)]
        mxn = xn
        hT_split = split_view("hT_split", xT_at, 2, ET, 128)
        x_tok = view(mtake(3 * D), 3, D)
        xn_tok = view(mtake(3 * D), 3, D)
        xe_split = split_view("xe_split", mtake(2 * D), 2, KT, 128)
        m_sig = [view(mtake(512), 512) for _ in range(2)]
        m_h = [view(mtake(512), 512) for _ in range(2)]
        ye = view(mtake(D), D)
        onehot = view(mtake(384), 3, 128)
        gated = view(mtake(384), 3, 128)
        gatedT = view(mtake(384), 3, 128)
        moe_const_at = mtake(256 + 3)
        tri, iota, real = view(moe_const_at, 128), view(moe_const_at + 128, 128), view(moe_const_at + 256, 3)
        logits = view(mtake(3 * NE), 3, NE)
        best = view(mtake(3 * 8), 3, 8)
        best_at = view(mtake(3 * 8), 3, 8).bitcast(U32)
        best_f = view(mtake(3 * 8), 3, 8)
        gap = view(mtake(3), 3, 1)
        gap_exp = view(mtake(3), 3, 1)
        gap_sum = view(mtake(3), 3, 1)
        gate1 = view(mtake(3), 3, 1)
        gate2 = view(mtake(3), 3, 1)
        hit1 = view(mtake(3 * NE), 3, NE)
        hit2 = view(mtake(3 * NE), 3, NE)
        gate_a = view(mtake(3 * NE), 3, NE)
        gate_b = view(mtake(3 * NE), 3, NE)
        chosen = view(mtake(3 * NE), 3, NE)
        place_1 = view(mtake(3 * NE), 3, NE)
        slot_of = view(mtake(3 * ITEMS), 3, ITEMS)
        gate_of = view(mtake(3 * ITEMS), 3, ITEMS)
        counts = view(mtake(NE), NE)
        flag_f = view(mtake(EXTRA), EXTRA)
        flag_sum = view(mtake(EXTRA), EXTRA)
        flags = view(mtake(3 * EXTRA), 3, EXTRA)
        flags_i = flags.bitcast(I32)

        def slot(c, ringlen=RING):
            return slots[c % ringlen]

        full = [sem(f"psum_full{b}") for b in range(8)]
        free = [sem(f"psum_free{b}") for b in range(8)]
        loaded = [sem(f"chunk_loaded{s}") for s in range(MRING)]
        raw_used = sem("cache_chunk_used")
        hi_ready = sem("chunk_high_ready")
        lo_ready = sem("chunk_low_ready")
        split_used = sem("split_chunk_used")
        small_loaded = sem("small_loaded")
        state_loaded = sem("state_loaded")
        wpool_loaded = sem("wpool_loaded")
        spread_loaded = sem("spread_table_loaded")
        moe_small = sem("moe_tables_loaded")
        ones_set = sem("constants_set")
        gain_ready = Tally(sem("gain_ready"), 2)
        sq_ready = Tally(sem("squares_ready"), 16)
        rstd_ready = Tally(sem("rstd_ready"), 2)
        xn_ready = Tally(sem("xn_ready"), 16)
        win_ready = Tally(sem("window_ready"), 1 + 2 + 3 + 4)
        mean_ready = Tally(sem("mean_ready"), 2 * PG)
        hsq_ready = Tally(sem("head_squares_ready"), 24)
        hrstd_ready = Tally(sem("head_rstd_ready"), 2)
        xh_ready = Tally(sem("xn_high_ready"), 16)
        xl_ready = Tally(sem("xn_low_ready"), 16)
        zeroed = Tally(sem("sample_tiles_zeroed"), 4)
        filled = Tally(sem("queries_placed"), 16 * HB)
        bh_ready = Tally(sem("branches_high_ready"), 2)
        bl_ready = Tally(sem("branches_low_ready"), 2)
        mh_ready = Tally(sem("merged_high_ready"), KT)
        ml_ready = Tally(sem("merged_low_ready"), KT)
        hh_ready = sem("hidden_high_ready")
        hl_ready = sem("hidden_low_ready")
        eh_ready = sem("expert_high_ready")
        gains_loaded = sem("gains_loaded")
        router_loaded = sem("router_loaded")
        max_ready = Tally(sem("max_ready"), 16)
        exp_ready = Tally(sem("exp_ready"), 16)
        rden_ready = Tally(sem("rden_ready"), 16)
        p_ready = Tally(sem("probs_ready"), 16)
        scored = Tally(sem("cache_scored"), (NT - 1) * HB)
        s_max = Tally(sem("s_max_ready"), HB)
        s_exp = Tally(sem("s_exp_ready"), HB)
        s_rden = Tally(sem("s_rden_ready"), HB)
        s_p = Tally(sem("s_probs_ready"), HB)
        merged_ready = Tally(sem("merged_ready"), KT)
        u_stored = sem("u_rows_stored")
        v_stored = sem("v_rows_stored")
        k_stored = [sem(f"k_stored{i}") for i in range(2)]
        copied = sem("state_copied")
        y_stored = sem("y_stored")
        route = sem("routing_steps")
        gap_done = sem("gap_exp_ready")
        flags_ready = sem("flags_ready")
        m_hot = sem("onehot_ready")
        combined = sem("all_combined")

        class Sec:

            def __init__(self, where, base, start=None):
                self.where, self.base, self.start = where, base, start

            def bank(self, job):
                return self.where[job][0]

            def ps(self, job):
                return psum[:, self.bank(job), :]

            def wait_free(self, e, job):
                b, u = self.where[job]
                e.wait_ge(free[b], self.base(b) + u + 1)

            def wait_full(self, e, job):
                b, u = self.where[job]
                e.wait_ge(full[b], self.base(b) + u + 1)

            def wait_read(self, e, job):
                b, u = self.where[job]
                e.wait_ge(free[b], self.base(b) + u + 2)

            def wait_before(self, e, bank):
                e.wait_ge(free[bank], self.base(bank) + self.start[bank] + 1)

            def freed(self, instruction, job):
                instruction.then_inc(free[self.where[job][0]], 1)

        def att_sec(L):
            return Sec(plans["att"][0], lambda b: L * layer_uses[b])

        pre = Sec(plans["pre"][0], lambda b: 0)
        dense_sec = Sec(plans["dense"][0], lambda b: 0)
        prep = Sec(mplans["prep"][0], lambda b: moe_start[b])

        def item_sec(seq, kind):
            steady, per = mplans["steady"][2], mplans["extra"][2]
            if kind in ("first", "steady"):
                return Sec(mplans[kind][0], (lambda b: moe_start[b] + (seq - 1) * steady[b]) if kind == "steady"
                           else (lambda b: moe_start[b]), mplans[kind][1])
            if kind == "last":
                return Sec(mplans[kind][0], lambda b: moe_start[b] + (NE - 3) * steady[b], mplans[kind][1])
            return Sec(mplans[kind][0], lambda b: moe_start[b] + (NE - 3) * steady[b] - NE * per[b] + seq * per[b],
                       mplans[kind][1])

        def wait_chunk(e, L, c):
            e.wait_ge(loaded[c % RING], 16 * (L * dmas_until(N_LAYER, c % RING) + dmas_until(c + 1, c % RING)))

        def wait_moe_chunk(e, seq, c):
            s = c % MRING
            before = dmas_until(N_LAYER, s) + dmas_until(N_ATT, s) if s < RING else 0
            e.wait_ge(loaded[s], 16 * (before + seq * (N_EXPERT // MRING) + c // MRING + 1))

        def wait_cache_scored(e, L, S, m):
            if m >= 0:
                half, n = m // NT, m % NT
                if n == NT - 1:
                    S.wait_full(e, ("ss", half))
                else:
                    e.wait_ge(scored.sem, scored.at(L, half * (NT - 1) + n + 1))

        def through_items(e, item):
            item(0, 0, "first")
            with e.Fori(1, NE - 1) as i:
                item(i, i, "steady")
            item(NE - 1, NE - 1, "last")

        def through_extras(e, item):
            e.wait_ge(flags_ready, 1)
            items = e.value_load(flags_i[0:1, 2, EXTRA - 1:EXTRA], min_val=NE, max_val=ITEMS)
            with e.If(items > NE):
                with e.Fori(0, EXTRA) as x:
                    flag = e.value_load(flags_i[0:1, 0, bass.ds(x, 1)], min_val=0, max_val=1)
                    seq = e.value_load(flags_i[0:1, 1, bass.ds(x, 1)], min_val=NE, max_val=ITEMS - 1)
                    with e.If(flag > 0):
                        item(x, seq, "extra")

        block = ctx.enter_context(nc.Block())

        @block.sync
        def _(e):
            for tt, (a, n) in enumerate(TT):
                src = io["x_prompt"][0, a:a + n, :] if tt < 2 else io["x_sample"].rearrange("b t d -> (b t) d")
                e.dma_start(x_raw[0:n, tt, :], src).then_inc(small_loaded, 16)
            e.dma_start(view(const_at, const_end - const_at), io["const_a"]).then_inc(small_loaded, 16)

            def send(L, c, parts):
                assert len(parts) == DMAS[c]
                before = L * N_LAYER + c - RING
                if before >= 0:
                    L0, c0 = divmod(before, N_LAYER)
                    if KINDS[c0] == "W":
                        e.wait_ge(lo_ready, L0 * NW_LAYER + W_OF[c0] + 1)
                    else:
                        e.wait_ge(raw_used, L0 * N_CACHE + c0 - C_CACHE + 1)
                for dst, src in parts:
                    e.dma_start(dst, src).then_inc(loaded[c % RING], 16)

            def columns(w, a):
                return w.rearrange("(k p) n -> p k n", p=PART)[:, :, a:a + 256]

            def send_attention(L):
                for c in range(N_IN):
                    send(L, c, [(view(slot(c), KT, 256), columns(io["w_in"][L], 256 * c))])
                c = C_CACHE
                for kv in range(2):
                    for half in range(HB):
                        b0 = half * BH
                        send(L, c, [(view(slot(c), BH, 512),
                                     io["cache_kv_g0"][L, b0:b0 + BH, :, kv].rearrange("b m h d -> m b (h d)"))])
                        c += 1
                        for g in (1, 2):
                            for b in range(b0, b0 + BH):
                                send(L, c, [(view(slot(c), DS, 512), io[f"cache_kv_g{g}"][L, b].rearrange(
                                    "(m r) v h d -> m r v (h d)", r=DIL[g])[:, 0:DS, kv])])
                                c += 1
                for i in range(KT // 2):
                    for b in range(2):
                        send(L, c, [(view(slot(c), KT, 256), columns(io["w_in"][L], IN_COLS - 2 * D + b * D + 256 * i))])
                        c += 1
                    dst = view(slot(c), 2, 4, 256)
                    send(L, c, [(dst[:, b], columns(io[name][L], 256 * i))
                                for b, name in enumerate(("w_branch_pool", "w_branch_attn"))])
                    c += 1
                for i in range(KT // 2):
                    send(L, c, [(view(slot(c), KT, 256), columns(io["w_out"][L], 256 * i))])
                    c += 1
                assert c == N_ATT

            def send_dense():
                for i in range(FT // 2):
                    for b, name in enumerate(("w1_dense", "w3_dense")):
                        c = C_UP + 2 * i + b
                        send(0, c, [(view(slot(c), KT, 256), columns(io[name][0], 256 * i))])
                w2 = io["w2_dense"][0].rearrange("(f p) n -> p f n", p=PART)
                for i in range(N_DOWN):
                    send(0, C_DOWN + i, [(view(slot(C_DOWN + i), 2, D), w2[:, 2 * i:2 * i + 2, :])])

            send_attention(0)
            send_dense()
            send_attention(1)

            def send_chunk(ex, seq, c):
                e.wait_ge(lo_ready, NW + seq * N_EXPERT + c - MRING + 1)
                if c < 28:
                    name, a = ("we_gate", "we_up")[c // 2 % 2], 512 * (c // 4) + 256 * (c % 2)
                    dst, src = view(slot(c, MRING), KT, 256), columns(io[name][0, ex], a)
                else:
                    dst = view(slot(c, MRING), 2, D)
                    src = io["we_down"][0, ex].rearrange("(f p) n -> p f n", p=PART)[:, 2 * (c - 28):2 * (c - 27), :]
                e.dma_start(dst, src).then_inc(loaded[c % MRING], 16)

            e.wait_ge(lo_ready, NW)
            for c in range(RING):
                send_chunk(0, 0, c)
            e.wait_ge(split_used, NW)
            e.wait_ge(v_stored, LAYERS * 16 * len(K_STORES))
            e.wait_ge(u_stored, LAYERS * 16 * U_STORES)
            e.wait_ge(copied, LAYERS * 16)
            for i in range(2):
                e.wait_ge(k_stored[i], LAYERS * 16 * (len(K_STORES) // 2))
            e.dma_start(view(moe_const_at, 259), io["const_m"]).then_inc(moe_small, 16)

            def send_item(ex, seq):
                for c in range(N_EXPERT):
                    send_chunk(ex, seq, c)

            for c in range(RING, N_EXPERT):
                send_chunk(0, 0, c)
            with e.Fori(1, NE) as i:
                send_item(i, i)
            through_extras(e, lambda x, seq, kind: send_item(x // (BLOCKS - 1), seq))
            e.wait_ge(combined, 1)
            for tt, (a, n) in enumerate(TT):
                dst = io["y_prompt"][0, a:a + n, :] if tt < 2 else io["y_sample"].rearrange("b t d -> (b t) d")
                e.dma_start(dst, x_tok[0:n, tt, :]).then_inc(y_stored, 16)
            e.wait_ge(y_stored, 48)

        @block.tensor
        def _(e):
            done = []

            def signal(r, inc):
                if inc is not None:
                    r.then_inc(inc, 1)
                elif done:
                    r.then_inc(done.pop(0), 1)

            def mm(out, lhsT, rhs, start, stop, inc=None, mixed=False):
                signal(e.matmul(out, lhsT, rhs, start=start, stop=stop, skip_group_check=mixed), inc)

            def mm3(out, lhsT, rhs, start, stop, inc=None):
                for n, (a, b) in enumerate(((0, 0), (0, 1), (1, 0))):
                    mm(out, lhsT[a], rhs[b], start and n == 0, stop and n == 2, inc if n == 2 else None)

            def turn(out, in_, inc=None):
                signal(e.transpose(out, in_, ident[0:in_.shape[0], 0:in_.shape[0]]), inc)

            def ssq(L, S, i):
                S.wait_free(e, ("ssq", i))
                for k in range(KT):
                    e.wait_ge(sq_ready.sem, sq_ready.at(L, 8 * i + k + 1))
                    mm(S.ps(("ssq", i))[:, 0:T], ones, work[:, k, :], k == 0, k == KT - 1,
                       full[S.bank(("ssq", i))] if k == KT - 1 else None)

            def chunk(L, w):
                e.wait_ge(lo_ready, L * NW_LAYER + w + 1)
                return w_split[(L * NW_LAYER + w) % SRING]

            def project(S, job, w, rhs, n=KT, normed=None):
                S.wait_free(e, job)
                for k in range(n):
                    if normed is not None:
                        e.wait_ge(xl_ready.sem, normed + k + 1)
                    mm3(S.ps(job)[:, 0:T], [w(0, k), w(1, k)], [rhs[:, 0, k, :], rhs[:, 1, k, :]], k == 0, k == n - 1,
                        full[S.bank(job)] if k == n - 1 else None)

            e.wait_ge(small_loaded, 64)
            for tt, (_, n) in enumerate(TT):
                for hf in range(2):
                    job = ("x", tt, hf)
                    pre.wait_free(e, job)
                    for i in range(4):
                        turn(pre.ps(job)[:, i * 128:i * 128 + n], x_raw[0:n, tt, (4 * hf + i) * 128:(4 * hf + i + 1) * 128],
                             full[pre.bank(job)] if i == 3 else None)
            e.wait_ge(gains_loaded, 16 * N_SMALL)
            pre.wait_free(e, ("gain", 0))
            turn(pre.ps(("gain", 0))[:, 0:LAYERS * N_GAIN], gain_raw[0:LAYERS * N_GAIN, :], full[pre.bank(("gain", 0))])
            e.wait_ge(ones_set, 3)

            def attention(L):
                S = att_sec(L)
                ssq(L, S, 0)

                def column_tile(job, c, normed=None):
                    w = chunk(L, c // 2).rearrange("p a (k n) -> p a k n", k=KT)
                    project(S, job, lambda a, k: w[:, a, k, 128 * (c % 2):128 * (c % 2 + 1)], xn_split, normed=normed)
                    if c % 2 == 1:
                        done.append(split_used)

                def head_sums(c):
                    job, i = ("hs", c // 12), c % 12
                    if i == 0:
                        S.wait_free(e, job)
                    e.wait_ge(hsq_ready.sem, hsq_ready.at(L, c + 1))
                    mm(S.ps(job)[0:HEADS, 0:T], band[:, HEADS - 2 * i:2 * HEADS - 2 * i], head_sq[:, c % 4, :],
                       i == 0, i == 11, full[S.bank(job)] if i == 11 else None)

                def spread(i):
                    return v_tok[0:HEADS, i // 4, 2, 128 * (i % 4):128 * (i % 4 + 1)]

                def head_factors(c):
                    job = ("bc", c)
                    S.wait_free(e, job)
                    if c == 0:
                        e.wait_ge(spread_loaded, 16 * (L + 1))
                    e.wait_ge(hrstd_ready.sem, hrstd_ready.at(L, c // 12 + 1))
                    mm(S.ps(job)[:, 0:T], spread(c % 12),
                       head_rms[0:HEADS, c // 12, :], True, True, full[S.bank(job)])

                def turn_rows(job, tile, a, n, count=4):
                    S.wait_free(e, job)
                    for i in range(count):
                        turn(S.ps(job)[0:n, 128 * i:128 * (i + 1)], tile(i)[:, a:a + n],
                             full[S.bank(job)] if i == count - 1 else None)

                for c in range(PG):
                    column_tile(("u", c), c, xl_ready.at(L, 0) if c == 0 else None)
                for n in range(36):
                    column_tile(column_job(n), PG + n)
                    if 2 <= n < 26:
                        head_sums(n - 2)
                    for job in AFTER.get(n, []):
                        kind, i = job[0:2]
                        if kind == "bc":
                            head_factors(i)
                        elif job == ("ut", 0):
                            S.wait_read(e, ("u", PG - 1))
                            turn_rows(job, lambda k: uflat[:, k, 16:16 + SEQ], SEQ - STATE, STATE)
                        elif job == ("ut", 1):
                            turn_rows(job, lambda k: u_new[:, k, :], 0, NS)
                        elif kind == "st":
                            S.wait_free(e, job)
                            e.wait_ge(state_loaded, 16 * (L + 1))
                            for k in range(PG):
                                turn(S.ps(job)[:, 120 * k:120 * (k + 1)], stateraw[0:120, 128 * k:128 * (k + 1)],
                                     full[S.bank(job)] if k == PG - 1 else None)
                        elif kind == "yp":
                            e.wait_ge(wpool_loaded, 16 * (L + 1))
                            S.wait_free(e, job)
                            e.wait_ge(mean_ready.sem, mean_ready.at(L, 2 * i + 2))
                            mm(S.ps(job)[:, 0:T], w_pool[:, i, :], pooled[:, i, :], True, True, full[S.bank(job)])
                        elif kind == "kt":
                            S.wait_read(e, ("bc", 12 + 4 * i + 3))
                            turn_rows(job, lambda k: kT[:, 4 * i + k, :], *TT[job[2]])
                        else:
                            S.wait_read(e, ("zv", 4 * i + 3))
                            turn_rows(job, lambda k: vT[i][:, k, :], *TT[job[2]])

                def scores(u):
                    j, qt, he = UNITS[u]
                    p = slice(64 * he, 64 * he + 64)
                    w = 128 * (qt + 1)
                    for n in range(1 + qt):
                        S.wait_free(e, ("S", u, n))
                    for g in range(G):
                        job = ("S", u, 1 if qt and g == 2 else 0)
                        last = g == 2 or (qt and g == 1)
                        at = 0 if qt and g == 2 else g * w
                        mm(S.ps(job)[:, at:at + w], qT[p, 4 * g + j, 128 * qt:128 * qt + 128],
                           kT[p, 4 * g + j, 0:w], True, True, full[S.bank(job)] if last else None)

                def turn_probs(u):
                    j, qt, he = UNITS[u]
                    e.wait_ge(p_ready.sem, p_ready.at(L, u + 1))
                    n = G * (qt + 1)
                    for i in range(n):
                        job = ("T", u, i // 4)
                        if i % 4 == 0:
                            S.wait_free(e, job)
                        turn(S.ps(job)[:, 128 * (i % 4):128 * (i % 4 + 1)], probs[u % 3][:, 128 * i:128 * (i + 1)],
                             full[S.bank(job)] if i == n - 1 or i % 4 == 3 else None)

                def values(u):
                    j, qt, he = UNITS[u]
                    job = ("O", j, qt)
                    if he == 0:
                        S.wait_free(e, job)
                    for n in range(1 + qt):
                        S.wait_read(e, ("T", u, n))
                    n = G * (qt + 1)
                    for i in range(n):
                        g, kt = i // (qt + 1), i % (qt + 1)
                        h = 2 * j + he
                        mm(S.ps(job)[64 * he:64 * he + 64, 0:128], v_tok[:, kt, g, 64 * h:64 * h + 64],
                           probsT[u % 2][:, 128 * i:128 * (i + 1)], i == 0, i == n - 1,
                           full[S.bank(job)] if he == 1 and i == n - 1 else None)

                def cache_tile(first_chunk, half, n):
                    where, i, g, b, t = TILES[n]
                    c = first_chunk + (1 + 2 * BH) * half + where
                    if n == 0 or TILES[n - 1][0] != where:
                        wait_chunk(e, L, c)
                    return view(slot(c) + 512 * i, 512)

                def release(n):
                    if n == NT - 1 or TILES[n + 1][0] != TILES[n][0]:
                        done.append(raw_used)

                def turn_cache(half, n):
                    job = ("kT", half, n)
                    tile = cache_tile(C_CACHE, half, n)
                    S.wait_free(e, job)
                    for j in range(J):
                        turn(S.ps(job)[:, 128 * j:128 * (j + 1)], tile[:, 128 * j:128 * (j + 1)],
                             full[S.bank(job)] if j == J - 1 else None)
                    release(n)

                def score_new(half):
                    job = ("ss", half)
                    S.wait_free(e, job)
                    e.wait_ge(filled.sem, filled.at(L, 16 * (half + 1)))
                    for g in range(G):
                        for j in range(J):
                            mm(S.ps(job)[:, 160 * g + 128:160 * (g + 1)],
                               q_all[:, 4 * g + j].rearrange("p b t h -> p (b t h)"), kT[:, 4 * g + j, SEQ:T],
                               g == 0 and j == 0, False, mixed=True)

                def score_cache(m):
                    half, n = m // NT, m % NT
                    _, _, g, b, t = TILES[n]
                    job = ("ss", half)
                    S.wait_read(e, ("kT", half, n))
                    for j in range(J):
                        inc = None
                        if j == J - 1:
                            inc = full[S.bank(job)] if n == NT - 1 else scored.sem
                        q = (q_all[:, j, b].rearrange("p t h -> p (t h)") if g == 0
                             else q_one[:, 4 * (g - 1) + j, DS * b + t, :])
                        mm(S.ps(job)[32 * b:32 * b + 32, 160 * g:160 * g + 128], q, cacheT[m % 3][:, j, :],
                           False, n == NT - 1 and j == J - 1, inc, mixed=True)

                def turn_s_probs(half):
                    e.wait_ge(s_p.sem, s_p.at(L, half + 1))
                    for name, lo, n in (("pt", 0, 128), ("pn", 128, NS)):
                        job = (name, half)
                        S.wait_free(e, job)
                        for g in range(G):
                            turn(S.ps(job)[0:n, 128 * g:128 * (g + 1)], s_probs[half][:, g, lo:lo + n],
                                 full[S.bank(job)] if g == G - 1 else None)

                LAG = 2

                def cache_step(m):
                    if m < HB * NT:
                        turn_cache(m // NT, m % NT)
                    if m in (LAG, NT + LAG):
                        score_new(m // NT)
                    if m >= LAG:
                        score_cache(m - LAG)
                    if m == NT + PT_AT:
                        turn_s_probs(0)

                S.wait_read(e, ("kt", 2, 2))
                S.wait_read(e, ("vt", 2, 2))
                for u in range(len(UNITS) + 3):
                    if u < len(UNITS):
                        scores(u)
                    if 2 <= u < len(UNITS) + 2:
                        turn_probs(u - 2)
                    if u >= 3:
                        values(u - 3)
                    for m in unit_tiles(u):
                        cache_step(m)
                for m in range(REST, HB * NT + LAG):
                    cache_step(m)

                def gather_heads(half):
                    job = ("ex", half)
                    S.wait_free(e, job)
                    S.wait_read(e, ("OS", half))
                    for j in range(J):
                        mm(S.ps(job)[:, 16 * j:16 * (j + 1)], o_own[:, 128 * j:128 * (j + 1)], pick, True, True,
                           full[S.bank(job)] if j == J - 1 else None)

                for half in range(HB):
                    job = ("OS", half)
                    S.wait_free(e, job)
                    S.wait_read(e, ("pt", half))
                    S.wait_read(e, ("pn", half))
                    for g in range(G):
                        mm(S.ps(job), sp_new[half][0:NS, g, :], v_tok[0:NS, 2, g, :], g == 0, False, mixed=True)
                    for n in range(NT):
                        _, _, g, b, t = TILES[n]
                        tile = cache_tile(C_CACHE + 2 * (1 + 2 * BH), half, n)
                        p = sp_all[half][:, b, :] if g == 0 else sp_one[half][:, g - 1, DS * b + t, :]
                        last = n == NT - 1
                        mm(S.ps(job)[32 * b:32 * b + 32], p, tile, False, last, full[S.bank(job)] if last else None, mixed=True)
                        release(n)
                        if half == 0 and n == PT1_AT:
                            turn_s_probs(1)
                        if half == 1 and n == EX_AT:
                            gather_heads(0)

                for i in range(KT // 2):
                    for b in range(2):
                        w = chunk(L, W_MERGE + 3 * i + b).rearrange("p a (k n) -> p a k n", k=KT)
                        for x in range(2):
                            project(S, (f"g{b}", 2 * i + x), lambda a, k: w[:, a, k, 128 * x:128 * (x + 1)], xn_split)
                        done.append(split_used)
                    if i == 0:
                        gather_heads(1)
                        e.wait_ge(bl_ready.sem, bl_ready.at(L, 2))
                    w = chunk(L, W_MERGE + 3 * i + 2).rearrange("p a (b k n) -> p a b k n", b=2, k=4)
                    for x in range(2):
                        for b in range(2):
                            project(S, (("pb", "ab")[b], 2 * i + x), lambda a, k: w[:, a, b, k, 128 * x:128 * (x + 1)],
                                    branch_split[:, b], 4)
                    done.append(split_used)
                e.wait_ge(ml_ready.sem, ml_ready.at(L, KT))
                for c in range(KT):
                    w = chunk(L, W_OUT + c // 2).rearrange("p a (k n) -> p a k n", k=KT)
                    project(S, ("wo", c), lambda a, k: w[:, a, k, 128 * (c % 2):128 * (c % 2 + 1)], merged_split)
                    if c % 2 == 1:
                        done.append(split_used)

            def ffn():
                S = dense_sec
                ssq(0, S, 1)
                for i in range(FT // 2):
                    for b in range(2):
                        w = chunk(0, W_UP + 2 * i + b).rearrange("p a (k n) -> p a k n", k=KT)
                        for x in range(2):
                            project(S, (("fa", "fb")[b], 2 * i + x), lambda a, k: w[:, a, k, 128 * x:128 * (x + 1)], xn_split,
                                    normed=xl_ready.at(0, KT) if (i, b, x) == (0, 0, 0) else None)
                        done.append(split_used)
                for f in range(FT):
                    w = chunk(0, W_DOWN + f // 2).rearrange("p a (f n) -> p a f n", f=2)
                    e.wait_ge(hl_ready, f + 1)
                    for n in range(KT):
                        job = ("fd", n)
                        if f == 0:
                            S.wait_free(e, job)
                        mm3(S.ps(job)[:, 0:T], [w[:, a, f % 2, 128 * n:128 * (n + 1)] for a in range(2)],
                            [hid_split[:, a, f, :] for a in range(2)], f == 0, f == FT - 1,
                            full[S.bank(job)] if f == FT - 1 else None)
                    if f % 2 == 1:
                        done.append(split_used)

            attention(0)
            ffn()
            attention(1)

            P = prep
            ssq(1, P, 1)
            assert not done
            for name, src in (("xt", xT), ("xnt", mxn)):
                for tt, (a, n) in enumerate(TT):
                    for hf in range(2):
                        job = (name, tt, hf)
                        P.wait_free(e, job)
                        if name == "xnt" and tt == 0:
                            e.wait_ge(xn_ready.sem, xn_ready.at(1, 8 + 4 * (hf + 1)))
                        for i in range(4):
                            turn(P.ps(job)[0:n, 128 * i:128 * (i + 1)], src[:, 4 * hf + i, a:a + n],
                                 full[P.bank(job)] if i == 3 else None)
            e.wait_ge(router_loaded, 32)
            for tt, (a, n) in enumerate(TT):
                job = ("rl", tt)
                P.wait_free(e, job)
                for k in range(KT):
                    mm(P.ps(job)[0:n, 0:NE], mxn[:, k, a:a + n], router[:, k, :], k == 0, False)
                mm(P.ps(job)[0:n, 0:NE], ones[0:1, 0:n], router_bias[0:1, :], False, True, full[P.bank(job)])
            e.wait_ge(route, R_CHOSEN)
            e.wait_ge(moe_small, 16)
            for tt in range(3):
                job = ("pos", tt)
                P.wait_free(e, job)
                for t2 in range(tt):
                    mm(P.ps(job)[:, 0:NE], ones, chosen[:, t2, :], t2 == 0, False)
                mm(P.ps(job)[:, 0:NE], tri, chosen[:, tt, :], tt == 0, True, full[P.bank(job)])
            P.wait_free(e, ("cnt", 0))
            for tt in range(3):
                mm(P.ps(("cnt", 0))[:, 0:NE], ones, chosen[:, tt, :], tt == 0, tt == 2,
                   full[P.bank(("cnt", 0))] if tt == 2 else None)
            P.wait_read(e, ("xnt", 2, 1))

            def gather(I, n):
                job = ("xe", n)
                I.wait_free(e, job)
                for k in range(4):
                    for tt, (_, nt) in enumerate(TT):
                        mm(I.ps(job)[:, 128 * k:128 * (k + 1)], xn_tok[0:nt, tt, 128 * (4 * n + k):128 * (4 * n + k + 1)],
                           onehot[0:nt, tt, :], tt == 0, tt == 2, full[I.bank(job)] if k == 3 and tt == 2 else None)

            e.wait_ge(m_hot, 6)
            gather(P, 0)
            gather(P, 1)

            def item(i, seq, kind):
                I = item_sec(seq, kind)
                ahead = kind in ("first", "steady")
                if kind == "extra":
                    e.wait_ge(m_hot, 6 * seq + 6)
                    gather(I, 0)
                    gather(I, 1)

                def wait_gathered(n):
                    if kind == "extra":
                        I.wait_read(e, ("xe", n))
                    else:
                        I.wait_before(e, PAIR[n])

                def turn_gates():
                    job = ("gst", 0)
                    I.wait_free(e, job)
                    for tt, (_, nt) in enumerate(TT):
                        turn(I.ps(job)[:, 128 * tt:128 * tt + nt], gated[0:nt, tt, :], full[I.bank(job)] if tt == 2 else None)

                def combine(name):
                    for tt, (_, nt) in enumerate(TT):
                        for hf in range(2):
                            job = (name, tt, hf)
                            I.wait_free(e, job)
                            mm(I.ps(job)[0:nt], gatedT[:, tt, 0:nt], ye[:, 512 * hf:512 * (hf + 1)], True, True,
                               full[I.bank(job)])

                def expert_chunk(v):
                    e.wait_ge(lo_ready, NW + seq * N_EXPERT + v + 1)
                    return e_split[v % MSRING]

                def turn_hidden(c):
                    job = ("ht", c)
                    I.wait_free(e, job)
                    I.wait_read(e, ("eu", c))
                    for i in range(4):
                        turn(I.ps(job)[:, 128 * i:128 * (i + 1)], m_h[c % 2][:, 128 * i:128 * (i + 1)],
                             full[I.bank(job)] if i == 3 else None)

                wait_gathered(0)
                for c in range(7):
                    for b in range(2):
                        job = (("eg", "eu")[b], c)
                        I.wait_free(e, job)
                        for x in range(2):
                            w = expert_chunk(4 * c + 2 * b + x).rearrange("p a (k n) -> p a k n", k=KT)
                            for k in range(KT):
                                if (c, b, x, k) == (0, 0, 0, KT // 2):
                                    wait_gathered(1)
                                mm3(I.ps(job)[:, 256 * x:256 * (x + 1)], [xe_split[:, a, k, :] for a in range(2)],
                                    [w[:, a, k, :] for a in range(2)], k == 0, k == KT - 1,
                                    full[I.bank(job)] if x == 1 and k == KT - 1 else None)
                            done.append(split_used)
                    if c >= 1:
                        turn_hidden(c - 1)
                    elif kind in ("steady", "last"):
                        for hf in range(2):
                            I.wait_before(e, mplans["first"][0][("ed", hf)][0])
                        combine("cb")
                    if c == 0 and ahead:
                        turn_gates()
                for hf in range(2):
                    I.wait_free(e, ("ed", hf))
                for f in range(ET):
                    if f % 2 == 0:
                        w = expert_chunk(28 + f // 2).rearrange("p a (f n) -> p a f n", f=2)
                    if f % 4 == 0:
                        I.wait_read(e, ("ht", f // 4))
                    for hf in range(2):
                        job = ("ed", hf)
                        mm3(I.ps(job), [hT_split[:, a, f, :] for a in range(2)],
                            [w[:, a, f % 2, 512 * hf:512 * (hf + 1)] for a in range(2)], f == 0, f == ET - 1,
                            full[I.bank(job)] if f == ET - 1 else None)
                    if f % 2 == 1:
                        done.append(split_used)
                    if f == 3:
                        turn_hidden(6)
                    if f == 15 and ahead:
                        e.wait_ge(m_hot, 6 * seq + 12)
                        gather(I, 0)
                if ahead:
                    gather(I, 1)
                else:
                    turn_gates()
                    I.wait_read(e, ("gst", 0))
                    I.wait_read(e, ("ed", 0))
                    I.wait_read(e, ("ed", 1))
                    combine("co")
                assert not done

            through_items(e, item)
            through_extras(e, item)

        @block.scalar
        def _(e):
            def copy(S, job, out, in_):
                S.wait_full(e, job)
                S.freed(e.activation(out, in_, ACT.Copy), job)

            def norm(L, S, i, w=None, after=None):
                for k in range(KT):
                    if after is not None:
                        after[0].wait_read(e, (after[1], k))
                    e.activation(work[:, k, :], xT[:, k, :], ACT.Square).then_inc(sq_ready.sem, 1)
                if w is not None:
                    split_high(L, w)
                S.wait_full(e, ("ssq", i))
                S.freed(e.activation(rms, S.ps(("ssq", i))[:, 0:T], ACT.Sqrt, bias=eps[:, 0:1], scale=1.0 / D), ("ssq", i))

            def split_high(L, w):
                c, gw = C_OF[w], L * NW_LAYER + w
                wait_chunk(e, L, c)
                if gw >= SRING:
                    e.wait_ge(split_used, gw - SRING + 1)
                e.activation(w_split[gw % SRING][:, 0, :], view(slot(c), CH), ACT.Copy).then_inc(hi_ready, 1)

            def split_norm(L, i):
                for k in range(KT):
                    e.wait_ge(xn_ready.sem, xn_ready.at(L, 8 * i + k + 1))
                    e.activation(xn_split[:, 0, k, :], xn[:, k, :], ACT.Copy).then_inc(xh_ready.sem, 1)

            at = 0
            for name in ("norm_attn", "norm_ffn", "pool_scale"):
                src = io[name].rearrange("l (k p) -> (l k) p", p=PART)
                e.dma_start(gain_raw[at:at + src.shape[0], :], src).then_inc(gains_loaded, 16)
                at += src.shape[0]
            for name in ("q_norm", "k_norm"):
                for he in range(2):
                    e.dma_start(gain_raw[at:at + LAYERS, 64 * he:64 * he + 64], io[name]).then_inc(gains_loaded, 16)
                at += LAYERS
            e.dma_start(router, io["router_w"][0].rearrange("(k p) n -> p k n", p=PART)).then_inc(router_loaded, 16)
            e.dma_start(router_bias[0:1, :], io["router_b"]).then_inc(router_loaded, 16)

            e.wait_ge(ones_set, 3)
            pre.wait_read(e, ("x", 2, 1))

            def attention(L):
                S = att_sec(L)
                if L == 0:
                    split_high(0, 0)
                norm(L, S, 0, 1, (dense_sec, "fd") if L else None)
                split_norm(L, 0)

                split_high(L, 2)
                for n in range(37):
                    if n % 2 == 0 and n // 2 + 3 < N_IN:
                        split_high(L, n // 2 + 3)
                    c = n - 1
                    if 0 <= c < 24:
                        if c == 20:
                            e.wait_ge(u_stored, 16 * U_STORES * (L + 1))
                        S.wait_full(e, ("z", c))
                        e.activation(head_sq[:, c % 4, :], S.ps(("z", c))[:, 0:T], ACT.Square).then_inc(hsq_ready.sem, 1)
                        S.freed(e.activation(qT[:, c, :] if c < 12 else kT[:, c - 12, :], S.ps(("z", c))[:, 0:T], ACT.Copy),
                                ("z", c))
                    elif c >= 24:
                        v = c - 24
                        copy(S, ("zv", v), vT[v // 4][:, v % 4, :], S.ps(("zv", v))[:, 0:T])
                    if c in (13, 25):
                        job = ("hs", (c - 13) // 12)
                        S.wait_full(e, job)
                        S.freed(e.activation(head_rms[0:HEADS, job[1], :], S.ps(job)[0:HEADS, 0:T], ACT.Sqrt,
                                             bias=eps[0:HEADS, 0:1], scale=1.0 / HD), job)
                    for job in AFTER.get(c, []):
                        if job[0] == "vt":
                            _, g, tt = job
                            count = TT[tt][1]
                            copy(S, job, v_tok[0:count, tt, g, :], S.ps(job)[0:count])

                def cache_copy(m):
                    if m == 0:
                        for i in range(2):
                            e.wait_ge(k_stored[i], 16 * (len(K_STORES) // 2) * (L + 1))
                    if m % 2 == 0:
                        wait_cache_scored(e, L, S, m - 3)
                        copy(S, ("kT", m // NT, m % NT), cacheT[m % 3], S.ps(("kT", m // NT, m % NT))
                             .rearrange("p (j m) -> p j m", j=J))

                for u in range(len(UNITS) + 3):
                    if 2 <= u < len(UNITS) + 2:
                        v = u - 2
                        for n in range(1 + UNITS[v][1]):
                            w = min(512, 128 * G * (UNITS[v][1] + 1) - 512 * n)
                            copy(S, ("T", v, n), probsT[v % 2][:, 512 * n:512 * n + w], S.ps(("T", v, n))[:, 0:w])
                    if u < len(UNITS):
                        w = 128 * G * (UNITS[u][1] + 1)
                        e.wait_ge(max_ready.sem, max_ready.at(L, u + 1))
                        e.activation(probs[u % 3][:, 0:w], probs[u % 3][:, 0:w], ACT.Exp, bias=stats[:, u:u + 1],
                                     accum_out=stats[:, 16 + u:17 + u]).then_inc(exp_ready.sem, 1)
                    for m in unit_tiles(u):
                        cache_copy(m)

                e.wait_ge(v_stored, 16 * len(K_STORES) * (L + 1))
                for m in range(REST, HB * NT):
                    cache_copy(m)
                    if m == NT + EXP_AT:
                        sample_exp(e, L, 0)
                    if m == NT + PT_AT + 2:
                        place_probs(e, L, S, 0)
                sample_exp(e, L, 1)
                place_probs(e, L, S, 1)
                split_high(L, W_MERGE)
                split_high(L, W_MERGE + 1)

                for i in range(KT // 2):
                    for b in range(2):
                        w = W_MERGE + 3 * i + b
                        if w > W_MERGE:
                            split_high(L, w + 1)
                        for x in range(2):
                            c = 2 * i + x
                            if c >= 2:
                                S.wait_read(e, (("pb", "ab")[b], c - 2))
                            S.wait_full(e, (f"g{b}", c))
                            S.freed(e.activation(gate[(2 * c + b) % 4], S.ps((f"g{b}", c))[:, 0:T], ACT.Sigmoid), (f"g{b}", c))
                    if i == 0:
                        S.wait_read(e, ("yp", PG - 1))
                        e.activation(branch_split[:, 0, 0], poolT, ACT.Copy).then_inc(bh_ready.sem, 1)
                        S.wait_read(e, ("ex", 1))
                        e.activation(branch_split[:, 1, 0], attT, ACT.Copy).then_inc(bh_ready.sem, 1)
                    split_high(L, W_MERGE + 3 * i + 3)
                    for c in ((2 * i - 2, 2 * i - 1) if i else ()):
                        merge_high(e, L, c)
                for c in range(KT - 2, KT):
                    merge_high(e, L, c)
                for w in range(W_OUT + 1, NW_ATT + (L == 0)):
                    split_high(L, w)
            def merge_high(e, L, c):
                e.wait_ge(merged_ready.sem, merged_ready.at(L, c + 1))
                e.activation(merged_split[:, 0, c, :], merged[:, c, :], ACT.Copy).then_inc(mh_ready.sem, 1)

            def sample_exp(e, L, half):
                e.wait_ge(s_max.sem, s_max.at(L, half + 1))
                flat = s_probs[half].rearrange("p g k -> p (g k)")
                e.activation(flat, flat, ACT.Exp, bias=stats[:, half:half + 1],
                             accum_out=stats[:, 16 + half:17 + half]).then_inc(s_exp.sem, 1)

            def place_probs(e, L, S, half):
                job = ("pt", half)
                S.wait_full(e, job)
                e.wait_ge(zeroed.sem, zeroed.at(L, 4))
                ps = S.ps(job)
                e.activation(sp_all[half].rearrange("p b r -> p (b r)"), ps[:, 0:128], ACT.Copy)
                for g in (1, 2):
                    one = view(sp_at[half] + ROWS + 512 * (g - 1), 512)
                    r = e.activation(strided(one, 0, (128, BH), (32 + H, DS), (1, H)),
                                     ps[:, 128 * g:128 * (g + 1)].rearrange("p (b t h) -> p b t h", b=BH, t=DS), ACT.Copy)
                S.freed(r, job)

            def ffn():
                S = dense_sec
                norm(0, S, 1, W_UP + 1, (att_sec(0), "wo"))
                split_norm(0, 1)

                def hidden_high(f):
                    S.wait_read(e, ("fb", f))
                    e.activation(hid_split[:, 0, f, :], hid[f % 4], ACT.Copy).then_inc(hh_ready, 1)

                for i in range(FT // 2):
                    if i >= 1:
                        split_high(0, W_UP + 2 * i + 1)
                        hidden_high(2 * i - 2)
                        hidden_high(2 * i - 1)
                    for f in (2 * i, 2 * i + 1):
                        if f >= 4:
                            S.wait_read(e, ("fb", f - 4))
                        S.wait_full(e, ("fa", f))
                        S.freed(e.activation(up_a[f % 4], S.ps(("fa", f))[:, 0:T], ACT.Silu), ("fa", f))
                    split_high(0, W_UP + 2 * i + 2)
                split_high(0, W_DOWN + 1)
                hidden_high(FT - 2)
                hidden_high(FT - 1)
                for w in range(W_DOWN + 2, NW_LAYER):
                    split_high(0, w)
                split_high(1, 0)

            attention(0)
            ffn()
            attention(1)

            P = prep
            norm(1, P, 1, after=(att_sec(1), "wo"))
            for tt, (_, n) in enumerate(TT):
                for hf in range(2):
                    job = ("xnt", tt, hf)
                    copy(P, job, xn_tok[0:n, tt, 512 * hf:512 * (hf + 1)], P.ps(job)[0:n])
            e.wait_ge(route, R_GAP)
            e.activation(gap_exp[:, :, 0], gap[:, :, 0], ACT.Exp).then_inc(gap_done, 1)

            e.wait_ge(split_used, NW)

            def expert_high(seq, v):
                wait_moe_chunk(e, seq, v)
                e.wait_ge(split_used, NW + seq * N_EXPERT + v - MSRING + 1)
                e.activation(e_split[v % MSRING][:, 0, :], view(slot(v, MRING), CH), ACT.Copy).then_inc(hi_ready, 1)

            def high(I, job, out):
                I.wait_full(e, job)
                e.activation(out, I.ps(job).rearrange("p (k s) -> p k s", k=4), ACT.Copy).then_inc(eh_ready, 1)

            def gathered_high(I, n):
                high(I, ("xe", n), xe_split[:, 0, 4 * n:4 * n + 4, :])

            expert_high(0, 0)
            expert_high(0, 1)
            gathered_high(P, 0)
            gathered_high(P, 1)

            def item(i, seq, kind):
                I = item_sec(seq, kind)
                ahead = kind in ("first", "steady")
                if kind == "extra":
                    expert_high(seq, 0)
                    expert_high(seq, 1)
                    gathered_high(I, 0)
                    gathered_high(I, 1)
                for c in range(7):
                    expert_high(seq, 4 * c + 2)
                    expert_high(seq, 4 * c + 3)
                    if c >= 2:
                        I.wait_read(e, ("eu", c - 2))
                    I.wait_full(e, ("eg", c))
                    I.freed(e.activation(m_sig[c % 2], I.ps(("eg", c)), ACT.Silu), ("eg", c))
                    expert_high(seq, 4 * c + 4)
                    expert_high(seq, 4 * c + 5)
                    if c >= 1:
                        high(I, ("ht", c - 1), hT_split[:, 0, 4 * c - 4:4 * c, :])
                for v in range(28, N_EXPERT):
                    if v + 2 < N_EXPERT or ahead:
                        expert_high(seq, v + 2)
                    if v == 29:
                        high(I, ("ht", 6), hT_split[:, 0, 24:28, :])
                    if v == 36 and ahead:
                        gathered_high(I, 0)
                I.wait_full(e, ("ed", 0))
                I.freed(e.activation(ye[:, 0:512], I.ps(("ed", 0)), ACT.Copy), ("ed", 0))
                if ahead:
                    gathered_high(I, 1)

            through_items(e, item)
            through_extras(e, item)

        @block.vector
        def _(e):
            def copy(S, job, out, in_):
                S.wait_full(e, job)
                S.freed(e.tensor_copy(out, in_), job)

            def split_low(L, w):
                c, gw = C_OF[w], L * NW_LAYER + w
                e.wait_ge(hi_ready, gw + 1)
                s = w_split[gw % SRING]
                e.tensor_tensor(s[:, 1, :], view(slot(c), CH), s[:, 0, :].bitcast(F32), ALU.subtract).then_inc(lo_ready, 1)

            def norm(L, S, i, w=None, split=True):
                if w is not None:
                    split_low(L, w)
                S.wait_read(e, ("ssq", i))
                e.reciprocal(rstd, rms).then_inc(rstd_ready.sem, 1)
                e.wait_ge(rstd_ready.sem, rstd_ready.at(L, i + 1))
                for k in range(KT + 1):
                    if k < KT:
                        e.scalar_tensor_tensor(out=xn[:, k, :], in0=xT[:, k, :], scalar=gain[:, 8 * i + k:8 * i + k + 1],
                                               in1=rstd, op0=ALU.mult, op1=ALU.mult).then_inc(xn_ready.sem, 1)
                    if k >= 1 and split:
                        e.wait_ge(xh_ready.sem, xh_ready.at(L, 8 * i + k))
                        e.tensor_tensor(xn_split[:, 1, k - 1, :], xn[:, k - 1, :], xn_split[:, 0, k - 1, :].bitcast(F32),
                                        ALU.subtract).then_inc(xl_ready.sem, 1)

            def add_to_x(S, name, tiles):
                for c in tiles:
                    job = (name, c)
                    S.wait_full(e, job)
                    S.freed(e.tensor_tensor(xT[:, c, :], xT[:, c, :], S.ps(job)[:, 0:T], ALU.add), job)

            def wait_x(S, name):
                for c in range(KT):
                    S.wait_read(e, (name, c))

            for b in range(8):
                e.sem_inc(free[b], 1)
            for tt, (a, n) in enumerate(TT):
                for hf in range(2):
                    job = ("x", tt, hf)
                    copy(pre, job, xT[:, 4 * hf:4 * hf + 4, a:a + n],
                         pre.ps(job).rearrange("p (k t) -> p k t", k=4)[:, :, 0:n])
            copy(pre, ("gain", 0), gains, pre.ps(("gain", 0))[:, 0:LAYERS * N_GAIN])
            pre.wait_read(e, ("gain", 0))
            pre.wait_read(e, ("x", 2, 1))
            u_all = uflat[:, :, 16 + SEQ:].rearrange("p g (b s) -> p g b s", b=DB)

            def attention(L):
                S = att_sec(L)
                at = 0
                for count in (KT, KT, PG, 1, 1):
                    r = e.tensor_copy(gain[:, at:at + count], gains[:, LAYERS * at + L * count:LAYERS * at + (L + 1) * count])
                    at += count
                r.then_inc(gain_ready.sem, 1)
                e.wait_ge(gain_ready.sem, gain_ready.at(L, 1))
                e.tensor_scalar(q_gain, gain[:, N_GAIN - 2:N_GAIN - 1], HD ** -0.5, None, ALU.mult).then_inc(gain_ready.sem, 1)
                e.wait_ge(gain_ready.sem, gain_ready.at(L, 2))
                if L == 0:
                    split_low(0, 0)
                norm(L, S, 0, 1)
                e.wait_ge(ones_set, 3 + L)
                for c in range(PG):
                    if c == 2:
                        split_low(L, 2)
                    job = ("u", c)
                    S.wait_full(e, job)
                    ps = S.ps(job)
                    e.tensor_copy(uflat[:, c, 16:16 + SEQ], ps[:, 0:SEQ])
                    e.tensor_copy(u_new[:, c, :], ps[:, SEQ:T])
                    S.freed(e.tensor_copy(u_all[:, c, :, STATE:], ps[:, SEQ:T].rearrange("p (b t) -> p b t", b=DB)), job)

                def mean(g):
                    steps = sum(range(1, g + 2))
                    e.wait_ge(win_ready.sem, win_ready.at(L, steps))
                    w = window[(steps - 1) % 2]
                    e.tensor_tensor(first_mean, w[:, 16:32], inv_count[:, g, :], ALU.mult).then_inc(mean_ready.sem, 1)
                    e.scalar_tensor_tensor(out=pooled[:, g, 16:SEQ], in0=w[:, 32:16 + SEQ], scalar=1.0 / WINDOWS[g],
                                           in1=uflat[:, g, 32:16 + SEQ], op0=ALU.mult, op1=ALU.subtract)
                    e.scalar_tensor_tensor(
                        out=pooled[:, g, SEQ:T].rearrange("p (b t) -> p b t", b=DB),
                        in0=w[:, 16 + SEQ:UW].rearrange("p (b s) -> p b s", b=DB)[:, :, STATE:], scalar=1.0 / WINDOWS[g],
                        in1=u_all[:, g, :, STATE:], op0=ALU.mult, op1=ALU.subtract)
                    e.wait_ge(mean_ready.sem, mean_ready.at(L, 2 * g + 1))
                    e.tensor_tensor(pooled[:, g, 0:16], first_mean, uflat[:, g, 16:32], ALU.subtract)\
                        .then_inc(mean_ready.sem, 1)

                rows = 0
                for n in range(37):
                    if n % 2 == 0 and n // 2 + 3 < N_IN:
                        split_low(L, n // 2 + 3)
                    c = n - 1
                    if c in (13, 25):
                        half = (c - 13) // 12
                        S.wait_read(e, ("hs", half))
                        e.reciprocal(head_rms[0:HEADS, half, :], head_rms[0:HEADS, half, :]).then_inc(hrstd_ready.sem, 1)
                    for job in AFTER.get(c, []):
                        kind, i = job[0:2]
                        if kind == "bc":
                            S.wait_full(e, job)
                            S.wait_read(e, ("z", i))
                            t, g = (qT[:, i, :], q_gain) if i < 12 else (kT[:, i - 12, :], gain[:, N_GAIN - 1:N_GAIN])
                            S.freed(e.scalar_tensor_tensor(out=t, in0=t, scalar=g, in1=S.ps(job)[:, 0:T],
                                                           op0=ALU.mult, op1=ALU.mult), job)
                        elif job == ("ut", 0):
                            copy(S, job, utok[0][0:STATE, :], S.ps(job)[0:STATE])
                        elif job == ("ut", 1):
                            copy(S, job, utok[1][0:NS, :], S.ps(job)[0:NS])
                        elif kind == "st":
                            S.wait_full(e, job)
                            for g in range(PG):
                                r = e.tensor_copy(u_all[:, g, :, 0:STATE], S.ps(job)[:, 120 * g:120 * (g + 1)]
                                                  .rearrange("p (b s) -> p b s", b=DB))
                            S.freed(r, job)
                        elif kind == "yp":
                            S.wait_full(e, job)
                            S.freed(e.tensor_scalar(poolT[:, i, :], S.ps(job)[:, 0:T], gain[:, 16 + i:17 + i], None, ALU.mult), job)
                        elif kind == "kt":
                            count = TT[job[2]][1]
                            if rows >= 2:
                                e.wait_ge(k_stored[rows % 2], 16 * (L * (len(K_STORES) // 2) + rows // 2))
                            copy(S, job, k_tok[0:count, rows % 2, :], S.ps(job)[0:count])
                            rows += 1
                    if c in MEAN_AT:
                        mean(MEAN_AT.index(c))

                def cache_copy(m):
                    if m == 1:
                        for i in range(2):
                            e.wait_ge(k_stored[i], 16 * (len(K_STORES) // 2) * (L + 1))
                    if m % 2 == 1:
                        wait_cache_scored(e, L, S, m - 3)
                        copy(S, ("kT", m // NT, m % NT), cacheT[m % 3], S.ps(("kT", m // NT, m % NT))
                             .rearrange("p (j m) -> p j m", j=J))

                for u in range(len(UNITS) + 3):
                    if u < len(UNITS):
                        j, qt, he = UNITS[u]
                        w = 128 * (qt + 1)
                        p = probs[u % 3]
                        for g in range(G):
                            n = 1 if qt and g == 2 else 0
                            at = 0 if n else g * w
                            if g == 0 or n:
                                S.wait_full(e, ("S", u, n))
                            r = e.scalar_tensor_tensor(out=p[:, g * w:(g + 1) * w], in0=dist[:, g, 256 - w:256],
                                                       scalar=-float(SLOPES[g, 2 * j + he]), in1=S.ps(("S", u, n))[:, at:at + w],
                                                       op0=ALU.mult, op1=ALU.add)
                            if g == 2 or (qt and g == 1):
                                S.freed(r, ("S", u, n))
                        for n in range(1 + qt):
                            S.wait_read(e, ("S", u, n))
                        e.tensor_reduce(stats[:, u:u + 1], p[:, 0:G * w], AX.X, ALU.max, negate=True).then_inc(max_ready.sem, 1)
                    if 1 <= u <= len(UNITS):
                        e.wait_ge(exp_ready.sem, exp_ready.at(L, u))
                        e.reciprocal(stats[:, 32 + u - 1:32 + u], stats[:, 16 + u - 1:16 + u]).then_inc(rden_ready.sem, 1)
                    if u >= 3 and UNITS[u - 3][2] == 1:
                        j, qt, _ = UNITS[u - 3]
                        copy(S, ("O", j, qt), attT[:, j, 128 * qt:128 * (qt + 1)], S.ps(("O", j, qt))[:, 0:128])
                    for m in unit_tiles(u):
                        cache_copy(m)

                def softmax_bias(half):
                    job = ("ss", half)
                    S.wait_full(e, job)
                    s = S.ps(job)[:, 0:G * 160].rearrange("p (g k) -> p g k", g=G)
                    p = s_probs[half]
                    e.tensor_tensor(p[:, :, 0:128], s[:, :, 0:128], bias_old, ALU.add)
                    S.freed(e.tensor_tensor(p[:, :, 128:160], s[:, :, 128:160], bias_new[:, half], ALU.add), job)
                    S.wait_read(e, job)
                    e.tensor_reduce(stats[:, half:half + 1], p.rearrange("p g k -> p (g k)"), AX.X, ALU.max, negate=True)\
                        .then_inc(s_max.sem, 1)

                def softmax_scale(half):
                    e.wait_ge(s_exp.sem, s_exp.at(L, half + 1))
                    e.reciprocal(stats[:, 32 + half:33 + half], stats[:, 16 + half:17 + half]).then_inc(s_rden.sem, 1)
                    e.wait_ge(s_rden.sem, s_rden.at(L, half + 1))
                    flat = s_probs[half].rearrange("p g k -> p (g k)")
                    e.tensor_scalar(flat, flat, stats[:, 32 + half:33 + half], None, ALU.mult).then_inc(s_p.sem, 1)

                def new_probs(half):
                    copy(S, ("pn", half), sp_new[half][0:NS], S.ps(("pn", half))[0:NS, 0:G * 128].rearrange("p (g r) -> p g r", g=G))

                def own_columns(half):
                    S.wait_full(e, ("OS", half))
                    S.freed(e.tensor_tensor(o_own, own_head, S.ps(("OS", half)), ALU.mult), ("OS", half))

                def sample_out(half):
                    at = SEQ + 16 * half
                    copy(S, ("ex", half), attT[:, :, at:at + 16], S.ps(("ex", half))[:, 0:64].rearrange("p (j s) -> p j s", j=J))

                e.wait_ge(v_stored, 16 * len(K_STORES) * (L + 1))
                for m in range(REST, HB * NT):
                    cache_copy(m)
                    if m == NT + MAX_AT:
                        softmax_bias(0)
                    if m == NT + SCALE_AT:
                        softmax_scale(0)
                    if m == NT + PT_AT + 1:
                        new_probs(0)
                softmax_bias(1)
                softmax_scale(1)
                new_probs(1)
                own_columns(0)
                sample_out(0)
                split_low(L, W_MERGE)
                split_low(L, W_MERGE + 1)
                own_columns(1)
                sample_out(1)

                for i in range(KT // 2):
                    if i >= 1:
                        split_low(L, W_MERGE + 3 * i + 1)
                    split_low(L, W_MERGE + 3 * i + 2)
                    if i == 0:
                        for b, src in enumerate((poolT, attT)):
                            e.wait_ge(bh_ready.sem, bh_ready.at(L, b + 1))
                            e.tensor_tensor(branch_split[:, b, 1], src, branch_split[:, b, 0].bitcast(F32), ALU.subtract)\
                                .then_inc(bl_ready.sem, 1)
                    split_low(L, W_MERGE + 3 * i + 3)
                    for x in range(2):
                        c = 2 * i + x
                        for b in range(2):
                            n = (2 * c + b) % 4
                            job = (("pb", "ab")[b], c)
                            if c >= 2:
                                e.wait_ge(merged_ready.sem, merged_ready.at(L, c - 1))
                            S.wait_read(e, (f"g{b}", c))
                            S.wait_full(e, job)
                            S.freed(e.tensor_tensor(prod[n], gate[n], S.ps(job)[:, 0:T], ALU.mult), job)
                for i in range(KT // 2):
                    if W_OUT + i + 1 < NW_ATT + (L == 0):
                        split_low(L, W_OUT + i + 1)
                    add_to_x(S, "wo", (2 * i, 2 * i + 1))
                wait_x(S, "wo")
                for i in range(2):
                    e.wait_ge(k_stored[i], 16 * (len(K_STORES) // 2) * (L + 1))

            def ffn():
                S = dense_sec
                norm(0, S, 1, W_UP + 1)
                for i in range(FT // 2):
                    if i >= 1:
                        split_low(0, W_UP + 2 * i + 1)
                    split_low(0, W_UP + 2 * i + 2)
                    for f in (2 * i, 2 * i + 1):
                        if f >= 4:
                            e.wait_ge(hl_ready, f - 3)
                        S.wait_read(e, ("fa", f))
                        S.wait_full(e, ("fb", f))
                        S.freed(e.tensor_tensor(hid[f % 4], up_a[f % 4], S.ps(("fb", f))[:, 0:T], ALU.mult), ("fb", f))
                for w in range(W_DOWN + 1, NW_LAYER):
                    split_low(0, w)
                split_low(1, 0)
                add_to_x(S, "fd", range(KT))
                wait_x(S, "fd")

            attention(0)
            ffn()
            attention(1)

            P = prep
            norm(1, P, 1, split=False)
            steps = {"n": 0}

            def step(instruction, wait=True):
                instruction.then_inc(route, 1)
                steps["n"] += 1
                if wait:
                    e.wait_ge(route, steps["n"])

            for tt, (_, n) in enumerate(TT):
                for hf in range(2):
                    job = ("xt", tt, hf)
                    copy(P, job, x_tok[0:n, tt, 512 * hf:512 * (hf + 1)], P.ps(job)[0:n])
            step(e.memset(logits, 0.0))
            for tt, (_, n) in enumerate(TT):
                copy(P, ("rl", tt), logits[0:n, tt, :], P.ps(("rl", tt))[0:n, 0:NE])
            for tt in range(3):
                P.wait_read(e, ("rl", tt))
            for tt in range(3):
                step(e.max(best[:, tt, :], logits[:, tt, :]), tt == 2)
            for tt in range(3):
                step(e.max_index(best_at[:, tt, :], best[:, tt, :], logits[:, tt, :]), tt == 2)
            step(e.tensor_copy(best_f, best_at))
            step(e.tensor_tensor(gap, best[:, :, 1:2], best[:, :, 0:1], ALU.subtract))
            assert steps["n"] == R_GAP
            e.wait_ge(gap_done, 1)
            step(e.tensor_scalar(gap_sum, gap_exp, 1.0, None, ALU.add))
            step(e.reciprocal(gate1, gap_sum))
            step(e.tensor_tensor(gate2, gap_exp, gate1, ALU.mult))
            e.wait_ge(moe_small, 16)
            for n, hit in enumerate((hit1, hit2)):
                for tt in range(3):
                    step(e.tensor_scalar(hit[:, tt, :], iota[:, 0:NE], best_f[:, tt, n:n + 1], real[:, tt:tt + 1],
                                         ALU.is_equal, ALU.mult), tt == 2)
            step(e.tensor_tensor(chosen, hit1, hit2, ALU.add))
            assert steps["n"] == R_CHOSEN
            for hit, gv, out in ((hit1, gate1, gate_a), (hit2, gate2, gate_b)):
                for tt in range(3):
                    step(e.tensor_scalar(out[:, tt, :], hit[:, tt, :], gv[:, tt, :], None, ALU.mult), tt == 2)

            def of_block(table, b):
                if b == 0:
                    return table[:, :, 0:NE]
                return table[:, :, NE:].rearrange("p t (e b) -> p t e b", b=BLOCKS - 1)[:, :, :, b - 1]

            for b in range(BLOCKS):
                step(e.tensor_tensor(of_block(gate_of, b), gate_a, gate_b, ALU.add), b == BLOCKS - 1)
            for tt in range(3):
                job = ("pos", tt)
                P.wait_full(e, job)
                P.freed(e.scalar_tensor_tensor(out=place_1[:, tt, :], in0=P.ps(job)[:, 0:NE], scalar=1.0,
                                               in1=chosen[:, tt, :], op0=ALU.add, op1=ALU.mult), job)
            copy(P, ("cnt", 0), counts, P.ps(("cnt", 0))[:, 0:NE])
            for tt in range(3):
                P.wait_read(e, ("pos", tt))
            P.wait_read(e, ("cnt", 0))
            for b in range(BLOCKS):
                step(e.tensor_scalar(of_block(slot_of, b), place_1, -(1.0 + 128 * b), None, ALU.add), b == BLOCKS - 1)

            def one_hots(i):
                for out, scale in ((onehot, False), (gated, True)):
                    for tt in range(3):
                        s1 = slot_of[:, tt, bass.ds(i, 1)]
                        if scale:
                            r = e.tensor_scalar(out[:, tt, :], iota, s1, gate_of[:, tt, bass.ds(i, 1)], ALU.is_equal, ALU.mult)
                        else:
                            r = e.tensor_scalar(out[:, tt, :], iota, s1, None, ALU.is_equal)
                        r.then_inc(m_hot, 1)

            def expert_low(seq, v):
                e.wait_ge(hi_ready, NW + seq * N_EXPERT + v + 1)
                w = e_split[v % MSRING]
                e.tensor_tensor(w[:, 1, :], view(slot(v, MRING), CH), w[:, 0, :].bitcast(F32), ALU.subtract)\
                    .then_inc(lo_ready, 1)

            def low(I, job, count, hi, out):
                e.wait_ge(eh_ready, count)
                I.freed(e.tensor_tensor(out, I.ps(job).rearrange("p (k s) -> p k s", k=4), hi.bitcast(F32), ALU.subtract), job)

            def gathered_low(I, n, count):
                low(I, ("xe", n), count, xe_split[:, 0, 4 * n:4 * n + 4, :], xe_split[:, 1, 4 * n:4 * n + 4, :])

            one_hots(0)
            expert_low(0, 0)
            expert_low(0, 1)
            gathered_low(P, 0, 1)
            gathered_low(P, 1, 2)
            for b in range(1, BLOCKS):
                step(e.tensor_scalar(flag_f.rearrange("p (e b) -> p e b", b=BLOCKS - 1)[:, :, b - 1], counts, 128.0 * b, None,
                                     ALU.is_gt), b == BLOCKS - 1)
            step(e.tensor_tensor_scan(flag_sum[0:1, :], ones[0:1, 0:EXTRA], flag_f[0:1, :], float(NE), ALU.mult, ALU.add))
            step(e.tensor_copy(flags_i[0:1, 0, :], flag_f[0:1, :]), False)
            step(e.tensor_copy(flags_i[0:1, 2, :], flag_sum[0:1, :]), False)
            e.tensor_tensor(flags_i[0:1, 1, :], flag_sum[0:1, :], flag_f[0:1, :], ALU.subtract).then_inc(flags_ready, 1)

            def item(i, seq, kind):
                I = item_sec(seq, kind)
                ahead = kind in ("first", "steady")
                highs = 9 * seq + 2

                def take_gates():
                    job = ("gst", 0)
                    I.wait_full(e, job)
                    g = I.ps(job).rearrange("p (t n) -> p t n", t=4)
                    e.tensor_copy(gatedT[:, 0:2, :], g[:, 0:2, :])
                    I.freed(e.tensor_copy(gatedT[:, 2, 0:NS], g[:, 2, 0:NS]), job)

                def add_rows(name):
                    for tt, (_, n) in enumerate(TT):
                        for hf in range(2):
                            job = (name, tt, hf)
                            x = x_tok[0:n, tt, 512 * hf:512 * (hf + 1)]
                            if (tt, hf) == (0, 0):
                                for bank in PAIR:
                                    I.wait_before(e, bank)
                            I.wait_full(e, job)
                            I.freed(e.tensor_tensor(x, x, I.ps(job)[0:n], ALU.add), job)

                if kind == "extra":
                    one_hots(NE + i)
                    expert_low(seq, 0)
                    expert_low(seq, 1)
                    gathered_low(I, 0, 9 * seq + 1)
                    gathered_low(I, 1, 9 * seq + 2)
                for c in range(7):
                    for v in range(4 * c + 2, 4 * c + 5):
                        expert_low(seq, v)
                    I.wait_read(e, ("eg", c))
                    I.wait_full(e, ("eu", c))
                    I.freed(e.tensor_tensor(m_h[c % 2], m_sig[c % 2], I.ps(("eu", c)), ALU.mult), ("eu", c))
                    expert_low(seq, 4 * c + 5)
                    if c >= 1:
                        low(I, ("ht", c - 1), highs + c, hT_split[:, 0, 4 * c - 4:4 * c, :], hT_split[:, 1, 4 * c - 4:4 * c, :])
                    elif kind in ("steady", "last"):
                        add_rows("cb")
                    if c == 0 and ahead:
                        take_gates()
                    if c == 3 and ahead:
                        one_hots(i + 1)
                for v in range(28, N_EXPERT):
                    if v + 2 < N_EXPERT or ahead:
                        expert_low(seq, v + 2)
                    if v == 29:
                        low(I, ("ht", 6), highs + 7, hT_split[:, 0, 24:28, :], hT_split[:, 1, 24:28, :])
                    if v == 36 and ahead:
                        gathered_low(I, 0, highs + 8)
                copy(I, ("ed", 1), ye[:, 512:D], I.ps(("ed", 1)))
                if ahead:
                    gathered_low(I, 1, highs + 9)
                else:
                    take_gates()
                    add_rows("co")

            through_items(e, item)
            last = item_sec(NE - 1, "last")
            for tt in range(3):
                for hf in range(2):
                    last.wait_read(e, ("co", tt, hf))
            through_extras(e, item)
            e.memset(stats[:, 0:1], 0.0).then_inc(combined, 1)

        @block.gpsimd
        def _(e):
            e.memset(ones, 1.0).then_inc(ones_set, 1)
            e.memset(eps, EPS).then_inc(ones_set, 1)
            e.memset(uflat, 0.0).then_inc(ones_set, 1)
            e.wait_ge(ones_set, 3)
            pre.wait_read(e, ("x", 2, 1))

            def attention(L):
                S = att_sec(L)
                e.dma_start(stateraw[0:DB * STATE, :], io["state_pool"][L].rearrange("b s c -> (b s) c")).then_inc(state_loaded, 16)
                e.dma_start(v_tok[0:HEADS, :, 2, :], io["spread"]).then_inc(spread_loaded, 16)
                e.dma_start(w_pool, io["w_pool"][L].rearrange("g c d -> c g d")).then_inc(wpool_loaded, 16)
                e.dma_start(io["pool_sample"][L, :, 0:STATE - DS, :], io["state_pool"][L, :, DS:STATE, :]).then_inc(copied, 16)

                S.wait_read(e, ("ut", 0))
                e.dma_start(io["pool_prompt"][L, 0], utok[0][0:STATE, :]).then_inc(u_stored, 16)
                S.wait_read(e, ("ut", 1))
                for b in range(DB):
                    e.dma_start(io["pool_sample"][L, b, STATE - DS:STATE, :], utok[1][DS * b:DS * (b + 1), :])\
                        .then_inc(u_stored, 16)

                S.wait_read(e, ("st", 0))
                n = 0
                for g in range(PG):
                    src = uflat[:, g, :]
                    if g >= 1:
                        e.wait_ge(mean_ready.sem, mean_ready.at(L, 2 * g))
                    for s in range(g + 1):
                        lo, back = 2 ** (s + 1) - 1, 2 ** s
                        dst = window[n % 2]
                        e.tensor_tensor(dst[:, lo:UW], src[:, lo:UW], src[:, lo - back:UW - back], ALU.add)\
                            .then_inc(win_ready.sem, 1)
                        n += 1
                        e.wait_ge(win_ready.sem, win_ready.at(L, n))
                        src = dst

                i = 0
                for n in sorted(ROW_TILES):
                    for kind, g, tt in (job for job in AFTER[n] if job[0] in ("kt", "vt")):
                        if kind == "kt":
                            S.wait_read(e, ("kt", g, tt))
                            store_rows(L, g, tt, 0, k_tok[:, i % 2, :], k_stored[i % 2])
                            i += 1
                        elif (g, tt) != (0, 0):
                            S.wait_read(e, ("vt", g, tt))
                            store_rows(L, g, tt, 1, v_tok[:, tt, g, :], v_stored)

                S.wait_read(e, ("vt", 2, 2))
                e.memset(view(strips_at, 12 * ROWS + 2 * J * BH * DS * 32), 0.0).then_inc(zeroed.sem, 1)

                def scale(u):
                    w = 128 * G * (UNITS[u][1] + 1)
                    e.wait_ge(rden_ready.sem, rden_ready.at(L, u + 1))
                    e.tensor_scalar(probs[u % 3][:, 0:w], probs[u % 3][:, 0:w], stats[:, 32 + u:33 + u], 1.0,
                                    ALU.mult, ALU.mult).then_inc(p_ready.sem, 1)

                def place_queries(half, he):
                    at = SEQ + 16 * half
                    p = slice(64 * he, 64 * he + 64)
                    for j in range(J):
                        h = 2 * j + he
                        src = qT.rearrange("p (g j) t -> p g j t", g=G)[p, :, j, at:at + 16]
                        e.tensor_copy(q_all.rearrange("p (g j) b t h -> p g j (b t) h", g=G)[p, :, j, :, h], src)\
                            .then_inc(filled.sem, 1)
                        one = view(q_one_at, 2 * J * BH * DS * 32)[p, :]
                        e.tensor_copy(strided(one, j * BH * DS * 32 + h, (J * BH * DS * 32, 2), (128, BH), (32 + H, DS)),
                                      src[:, 1:G].rearrange("p g (b t) -> p g b t", b=BH)).then_inc(filled.sem, 1)
                    e.wait_ge(filled.sem, filled.at(L, 16 * half + 8 * he + 8))

                for u in range(len(UNITS)):
                    scale(u)
                    if u == 0:
                        e.wait_ge(zeroed.sem, zeroed.at(L, 1))
                    if u < 2:
                        e.wait_ge(p_ready.sem, p_ready.at(L, u + 1))
                        place_queries(0, u)
                S.wait_read(e, ("O", J - 1, 1))
                e.wait_ge(v_stored, 16 * len(K_STORES) * (L + 1))
                for a in sp_at:
                    e.memset(view(a + ROWS, 1024), 0.0).then_inc(zeroed.sem, 1)
                e.memset(stats[:, 46:47], 0.0).then_inc(zeroed.sem, 1)
                e.wait_ge(zeroed.sem, zeroed.at(L, 4))
                S.wait_full(e, ("ss", 0))
                place_queries(1, 0)
                place_queries(1, 1)
                for c in range(KT):
                    if c == 0:
                        S.wait_full(e, ("ss", 1))
                    for b in range(2):
                        S.wait_read(e, (("pb", "ab")[b], c))
                    e.tensor_tensor(merged[:, c, :], prod[(2 * c) % 4], prod[(2 * c + 1) % 4], ALU.add)\
                        .then_inc(merged_ready.sem, 1)
                    if c >= 2:
                        merge_low(L, c - 2)
                merge_low(L, KT - 2)
                merge_low(L, KT - 1)
                S.wait_read(e, ("wo", KT - 1))

            def merge_low(L, c):
                e.wait_ge(mh_ready.sem, mh_ready.at(L, c + 1))
                e.tensor_tensor(merged_split[:, 1, c, :], merged[:, c, :], merged_split[:, 0, c, :].bitcast(F32), ALU.subtract)\
                    .then_inc(ml_ready.sem, 1)

            def store_rows(L, g, tt, kv, rows, signal):
                a, n = TT[tt]
                if tt == 2:
                    dst = io[f"kv{g}_sample"][L].rearrange("b t v h d -> (b t) v (h d)")[:, kv]
                else:
                    keep = min(SPAN[g], SEQ)
                    a -= SEQ - keep
                    dst = io[f"kv{g}_prompt"][L, 0, a:a + n, kv].rearrange("t h d -> t (h d)")
                e.dma_start(dst, rows[0:n, :]).then_inc(signal, 16)

            def ffn():
                for f in range(FT):
                    e.wait_ge(hh_ready, f + 1)
                    e.tensor_tensor(hid_split[:, 1, f, :], hid[f % 4], hid_split[:, 0, f, :].bitcast(F32), ALU.subtract)\
                        .then_inc(hl_ready, 1)
                for c in range(KT):
                    dense_sec.wait_read(e, ("fd", c))
                e.memset(uflat, 0.0).then_inc(ones_set, 1)

            attention(0)
            ffn()
            attention(1)


_INS = ["x_prompt", "x_sample", "state_pool", "cache_kv_g0", "cache_kv_g1", "cache_kv_g2", "norm_attn", "w_in", "q_norm",
        "k_norm", "w_pool", "pool_scale", "w_branch_pool", "w_branch_attn", "w_out", "norm_ffn", "w1_dense", "w3_dense",
        "w2_dense", "router_w", "router_b", "we_gate", "we_up", "we_down"]
_OUTS = [("y_prompt", (1, SEQ, D)), ("y_sample", (DB, DS, D)), ("pool_prompt", (LAYERS, 1, STATE, POOL_W)),
         ("pool_sample", (LAYERS, DB, STATE, POOL_W))]
for _g in range(G):
    _OUTS += [(f"kv{_g}_prompt", (LAYERS, 1, min(SPAN[_g], SEQ), 2, H, HD)), (f"kv{_g}_sample", (LAYERS, DB, DS, 2, H, HD))]


def kernel(**inputs):
    import concourse.bacc as bacc
    from concourse.bass_utils import run_bass_kernel_spmd

    nc = bacc.Bacc("TRN2", target_bir_lowering=False, num_devices=1)
    const_a, const_m, spread = shape_constants()
    arrays = {"in_" + n: np.ascontiguousarray(inputs[n]) for n in _INS}
    arrays["in_const_a"], arrays["in_const_m"], arrays["in_spread"] = const_a, const_m, spread
    io = {n[3:]: nc.dram_tensor(n, a.shape, mybir.dt.from_np(a.dtype), kind="ExternalInput").ap() for n, a in arrays.items()}
    for name, shape in _OUTS:
        io[name] = nc.dram_tensor("out_" + name, shape, F32, kind="ExternalOutput").ap()
    build(nc, io)
    r = run_bass_kernel_spmd(nc, [arrays], core_ids=[0])
    return tuple(r.results[0]["out_" + name] for name, _ in _OUTS)
```
